# Optimizing a Trainium2 kernel written in Bass

```python
import math
import jax, jax.numpy as jnp
from jax import lax
import numpy as np

D_MODEL = 1024
BATCH = 1
SEQ = 256
DEPTH = 2

HEAD_DIM = 64
ATTN_Q_HEADS = D_MODEL // (2 * HEAD_DIM)
ATTN_KV_HEADS = max(1, ATTN_Q_HEADS // 4)
RET_HEADS = D_MODEL // (2 * HEAD_DIM)
ATTN_WIDTH = ATTN_Q_HEADS * HEAD_DIM
KV_WIDTH = ATTN_KV_HEADS * HEAD_DIM
RET_WIDTH = RET_HEADS * HEAD_DIM
MIX_WIDTH = ATTN_WIDTH + RET_WIDTH
IN_SPLITS = (ATTN_WIDTH,
             ATTN_WIDTH + KV_WIDTH,
             ATTN_WIDTH + 2 * KV_WIDTH,
             ATTN_WIDTH + 2 * KV_WIDTH + RET_WIDTH,
             ATTN_WIDTH + 2 * KV_WIDTH + 2 * RET_WIDTH,
             ATTN_WIDTH + 2 * KV_WIDTH + 3 * RET_WIDTH)
IN_WIDTH = ATTN_WIDTH + 2 * KV_WIDTH + 4 * RET_WIDTH
WINDOW = 128
ATTN_BLOCK = 128
RET_CHUNK = 128
ROPE_THETA = 10000.0
RET_THETA = 10000.0
D_FF = ((8 * D_MODEL // 3 + 127) // 128) * 128
LN_EPS = 1e-5
GN_EPS = 1e-6
DEEPNORM_ALPHA = (2 * DEPTH) ** 0.25
DEEPNORM_BETA = (8 * DEPTH) ** -0.25


def layer_norm(x, g, b):
    xf = x.astype(jnp.float32)
    mu = jnp.mean(xf, axis=-1, keepdims=True)
    var = jnp.mean(jnp.square(xf - mu), axis=-1, keepdims=True)
    return ((xf - mu) * lax.rsqrt(var + LN_EPS)).astype(x.dtype) * g + b

def swiglu_ffn(x, w_gu, w_down):
    a, u = jnp.split(x @ w_gu, 2, axis=-1)
    return (jax.nn.silu(a) * u) @ w_down

def rope_tables(seq):
    pos = jnp.arange(seq, dtype=jnp.float32)
    inv_freq = ROPE_THETA ** (-jnp.arange(0, HEAD_DIM, 2, dtype=jnp.float32) / HEAD_DIM)
    ang = pos[:, None] * inv_freq[None, :]
    return jnp.cos(ang), jnp.sin(ang)

def retention_rotation_tables(seq):
    pos = jnp.arange(seq, dtype=jnp.float32)
    ang_freq = 1.0 / (RET_THETA ** jnp.linspace(0.0, 1.0, HEAD_DIM // 2, dtype=jnp.float32))
    ang = pos[:, None] * ang_freq[None, :]
    return jnp.cos(ang), jnp.sin(ang)

def apply_rope(x, cos, sin):
    c = cos[:, None, :].astype(x.dtype)
    s = sin[:, None, :].astype(x.dtype)
    x1, x2 = jnp.split(x, 2, axis=-1)
    return jnp.concatenate([x1 * c - x2 * s, x2 * c + x1 * s], axis=-1)

def apply_pair_rotation(x, cos, sin):
    c = cos[:, None, :].astype(x.dtype)
    s = sin[:, None, :].astype(x.dtype)
    xe = x[..., 0::2]
    xo = x[..., 1::2]
    return jnp.stack([xe * c - xo * s, xo * c + xe * s], axis=-1).reshape(x.shape)

def sliding_window_sink_attention(q, k, v, sinks):
    B, S, Hq, D = q.shape
    Hkv = k.shape[2]
    G = Hq // Hkv
    C = ATTN_BLOCK
    N = S // C
    qb = (q * (HEAD_DIM ** -0.5)).reshape(B, N, C, Hkv, G, D)

    def with_prev_block(t):
        tb = t.reshape(B, N, C, Hkv, D)
        prev = jnp.pad(tb, ((0, 0), (1, 0), (0, 0), (0, 0), (0, 0)))[:, :-1]
        return jnp.concatenate([prev, tb], axis=2)

    kk = with_prev_block(k)
    vv = with_prev_block(v)
    s = jnp.einsum('bnqhgd,bnkhd->bnhgqk', qb, kk).astype(jnp.float32)
    q_idx = jnp.arange(C)[:, None]
    k_rel = jnp.arange(2 * C)[None, :] - C
    rel = q_idx - k_rel
    band = (rel >= 0) & (rel < WINDOW)
    valid = (jnp.arange(N)[:, None] * C + k_rel) >= 0
    mask = band[None, :, :] & valid[:, None, :]
    s = jnp.where(mask[None, :, None, None, :, :], s, -jnp.inf)
    sink = sinks.astype(jnp.float32).reshape(Hkv, G)[None, None, :, :, None, None]
    m = jnp.maximum(jnp.max(s, axis=-1, keepdims=True), sink)
    p = jnp.exp(s - m)
    denom = jnp.sum(p, axis=-1, keepdims=True) + jnp.exp(sink - m)
    o = jnp.einsum('bnhgqk,bnkhd->bnqhgd', (p / denom).astype(v.dtype), vv)
    return o.reshape(B, S, Hq * D)

def multiscale_retention(q, k, v, gate):
    B, S, H, D = q.shape
    C = RET_CHUNK
    N = S // C
    log_gamma = jnp.log1p(-jnp.exp2(-5.0 - jnp.arange(H, dtype=jnp.float32)))
    idx = jnp.arange(C, dtype=jnp.float32)
    diff = idx[:, None] - idx[None, :]
    decay = jnp.where(diff[None] >= 0,
                      jnp.exp(jnp.maximum(diff, 0.0)[None] * log_gamma[:, None, None]), 0.0)
    w_k = jnp.exp((C - 1.0 - idx)[None, :] * log_gamma[:, None])
    w_q = jnp.exp((idx + 1.0)[None, :] * log_gamma[:, None])
    g_chunk = jnp.exp(C * log_gamma)
    qc = q.reshape(B, N, C, H, D)
    kc = k.reshape(B, N, C, H, D)
    vc = v.reshape(B, N, C, H, D)
    scores = jnp.einsum('bnihd,bnjhd->bnhij', qc, kc) * decay
    intra = jnp.einsum('bnhij,bnjhe->bnihe', scores, vc)
    kv = jnp.einsum('bnjhd,hj,bnjhe->bnhde', kc, w_k, vc)

    def step(state, kv_n):
        return state * g_chunk[None, :, None, None] + kv_n, state

    init = jnp.zeros((B, H, D, D), dtype=kv.dtype)
    _, states = lax.scan(step, init, jnp.moveaxis(kv, 1, 0))
    states = jnp.moveaxis(states, 0, 1)
    cross = jnp.einsum('bnihd,hi,bnhde->bnihe', qc, w_q, states)
    o = (intra + cross).reshape(B, S, H, D).astype(jnp.float32)
    mu = jnp.mean(o, axis=-1, keepdims=True)
    var = jnp.mean(jnp.square(o - mu), axis=-1, keepdims=True)
    o = ((o - mu) * lax.rsqrt(var + GN_EPS)).reshape(B, S, H * D).astype(gate.dtype)
    return jax.nn.silu(gate) * o

def hybrid_mixer(x, w_in, w_out, sinks, rope_cos, rope_sin, ret_cos, ret_sin):
    B, S, _ = x.shape
    h = x @ w_in
    qa, ka, va, qr, kr, vr, gr = jnp.split(h, IN_SPLITS, axis=-1)
    qa = apply_rope(qa.reshape(B, S, ATTN_Q_HEADS, HEAD_DIM), rope_cos, rope_sin)
    ka = apply_rope(ka.reshape(B, S, ATTN_KV_HEADS, HEAD_DIM), rope_cos, rope_sin)
    va = va.reshape(B, S, ATTN_KV_HEADS, HEAD_DIM)
    y_attn = sliding_window_sink_attention(qa, ka, va, sinks)
    qr = apply_pair_rotation(qr.reshape(B, S, RET_HEADS, HEAD_DIM), ret_cos, ret_sin)
    kr = apply_pair_rotation(kr.reshape(B, S, RET_HEADS, HEAD_DIM), ret_cos, ret_sin) * (HEAD_DIM ** -0.5)
    y_ret = multiscale_retention(qr, kr, vr.reshape(B, S, RET_HEADS, HEAD_DIM), gr)
    return jnp.concatenate([y_attn, y_ret], axis=-1) @ w_out

def first_inputs(seed: int = 0) -> dict:
    key = jax.random.key(seed)
    ks = jax.random.split(key, 16)
    f32 = jnp.float32
    x = jax.random.normal(ks[0], (BATCH, SEQ, D_MODEL), f32)
    col_scale = jnp.concatenate([
        jnp.ones((ATTN_WIDTH + KV_WIDTH,), f32),
        jnp.full((KV_WIDTH,), DEEPNORM_BETA, f32),
        jnp.ones((2 * RET_WIDTH,), f32),
        jnp.full((RET_WIDTH,), DEEPNORM_BETA, f32),
        jnp.ones((RET_WIDTH,), f32)])
    w_in = jax.random.normal(ks[1], (DEPTH, D_MODEL, IN_WIDTH), f32) * (D_MODEL ** -0.5) * col_scale
    w_out = jax.random.normal(ks[2], (DEPTH, MIX_WIDTH, D_MODEL), f32) * (MIX_WIDTH ** -0.5) * DEEPNORM_BETA
    attn_sinks = 0.5 * jax.random.normal(ks[3], (DEPTH, ATTN_Q_HEADS), f32)
    ffn1_w_gu = jax.random.normal(ks[4], (DEPTH, D_MODEL, 2 * D_FF), f32) * (D_MODEL ** -0.5) * DEEPNORM_BETA
    ffn1_w_down = jax.random.normal(ks[5], (DEPTH, D_FF, D_MODEL), f32) * (D_FF ** -0.5) * DEEPNORM_BETA
    ffn2_w_gu = jax.random.normal(ks[6], (DEPTH, D_MODEL, 2 * D_FF), f32) * (D_MODEL ** -0.5) * DEEPNORM_BETA
    ffn2_w_down = jax.random.normal(ks[7], (DEPTH, D_FF, D_MODEL), f32) * (D_FF ** -0.5) * DEEPNORM_BETA
    ln1_g = 1.0 + 0.02 * jax.random.normal(ks[8], (DEPTH, D_MODEL), f32)
    ln1_b = 0.02 * jax.random.normal(ks[9], (DEPTH, D_MODEL), f32)
    ln2_g = 1.0 + 0.02 * jax.random.normal(ks[10], (DEPTH, D_MODEL), f32)
    ln2_b = 0.02 * jax.random.normal(ks[11], (DEPTH, D_MODEL), f32)
    ln3_g = 1.0 + 0.02 * jax.random.normal(ks[12], (DEPTH, D_MODEL), f32)
    ln3_b = 0.02 * jax.random.normal(ks[13], (DEPTH, D_MODEL), f32)
    return {"x": x, "w_in": w_in, "w_out": w_out, "attn_sinks": attn_sinks,
            "ffn1_w_gu": ffn1_w_gu, "ffn1_w_down": ffn1_w_down,
            "ffn2_w_gu": ffn2_w_gu, "ffn2_w_down": ffn2_w_down,
            "ln1_g": ln1_g, "ln1_b": ln1_b, "ln2_g": ln2_g, "ln2_b": ln2_b,
            "ln3_g": ln3_g, "ln3_b": ln3_b}

def first_block(x, w_in, w_out, attn_sinks, ffn1_w_gu, ffn1_w_down, ffn2_w_gu, ffn2_w_down,
              ln1_g, ln1_b, ln2_g, ln2_b, ln3_g, ln3_b):
    S = x.shape[1]
    rope_cos, rope_sin = rope_tables(S)
    ret_cos, ret_sin = retention_rotation_tables(S)
    for l in range(DEPTH):
        x = layer_norm(DEEPNORM_ALPHA * x + 0.5 * swiglu_ffn(x, ffn1_w_gu[l], ffn1_w_down[l]),
                       ln1_g[l], ln1_b[l])
        x = layer_norm(DEEPNORM_ALPHA * x + hybrid_mixer(x, w_in[l], w_out[l], attn_sinks[l],
                                                         rope_cos, rope_sin, ret_cos, ret_sin),
                       ln2_g[l], ln2_b[l])
        x = layer_norm(DEEPNORM_ALPHA * x + 0.5 * swiglu_ffn(x, ffn2_w_gu[l], ffn2_w_down[l]),
                       ln3_g[l], ln3_b[l])
    return x


A_HEADS = 6
A_NOPE = 64
A_ROPE = 32
A_V = 64
Q_LORA = 768
KV_LORA = 256
B_HEADS = 6
DILATED_PATTERNS = ((128, 1), (512, 4), (2048, 16))
C_HEADS = 4
IDX_HEADS = 8
IDX_DIM = 64
TOPK_MAX = 256
Q_BLOCK = 128

A_WIDTH = A_HEADS * A_V
B_WIDTH = B_HEADS * HEAD_DIM
C_WIDTH = C_HEADS * HEAD_DIM
MIX_WIDTH_2 = A_WIDTH + B_WIDTH + C_WIDTH
N_ALIBI = B_HEADS + C_HEADS

SPLIT_SIZES = (Q_LORA, KV_LORA, A_ROPE,
               B_WIDTH, B_WIDTH, B_WIDTH,
               C_WIDTH, C_WIDTH, C_WIDTH,
               IDX_HEADS * IDX_DIM, IDX_DIM, IDX_HEADS,
               MIX_WIDTH_2)
IN_WIDTH_2 = sum(SPLIT_SIZES)
SPLIT_POINTS = [int(v) for v in np.cumsum(SPLIT_SIZES)[:-1]]

ALPHA = (2 * DEPTH) ** 0.25
BETA = (8 * DEPTH) ** -0.25


F32 = jnp.float32

def layer_norm_2(x, g, b, eps=1e-5):
    xf = x.astype(F32)
    mu = jnp.mean(xf, axis=-1, keepdims=True)
    xc = xf - mu
    var = jnp.mean(xc * xc, axis=-1, keepdims=True)
    return (xc * lax.rsqrt(var + eps) * g.astype(F32) + b.astype(F32)).astype(x.dtype)

def rms_norm(x, g, eps=1e-6):
    xf = x.astype(F32)
    ms = jnp.mean(xf * xf, axis=-1, keepdims=True)
    return (xf * lax.rsqrt(ms + eps) * g.astype(F32)).astype(x.dtype)

def apply_rope_2(x, cos, sin):
    half = x.shape[-1] // 2
    x1, x2 = x[..., :half].astype(F32), x[..., half:].astype(F32)
    return jnp.concatenate([x1 * cos - x2 * sin, x1 * sin + x2 * cos], axis=-1).astype(x.dtype)

def alibi_slopes():
    return 2.0 ** (-8.0 * jnp.arange(1, N_ALIBI + 1, dtype=F32) / N_ALIBI)

def to_blocks(a):
    b, s = a.shape[0], a.shape[1]
    return a.reshape((b, s // Q_BLOCK, Q_BLOCK) + a.shape[2:]).swapaxes(0, 1)

def from_blocks(a):
    a = a.swapaxes(0, 1)
    return a.reshape((a.shape[0], a.shape[1] * a.shape[2]) + a.shape[3:])

def mla_attention(q_nope, q_rope, k_nope, k_rope, v):
    s_len = q_nope.shape[1]
    nb = s_len // Q_BLOCK
    scale = (A_NOPE + A_ROPE) ** -0.5
    key_pos = jnp.arange(s_len)

    def block(args):
        qn, qr, start = args
        qpos = start + jnp.arange(Q_BLOCK)
        s = (jnp.einsum('bqhd,bshd->bhqs', qn, k_nope, preferred_element_type=F32)
             + jnp.einsum('bqhr,bsr->bhqs', qr, k_rope, preferred_element_type=F32)) * scale
        s = jnp.where(key_pos[None, :] <= qpos[:, None], s, -jnp.inf)
        p = jax.nn.softmax(s, axis=-1)
        return jnp.einsum('bhqs,bshd->bqhd', p.astype(v.dtype), v)

    out = lax.map(block, (to_blocks(q_nope), to_blocks(q_rope), jnp.arange(nb) * Q_BLOCK))
    return from_blocks(out)

def dilated_attention(q, k, v, slopes):
    bsz, s_len, nh, dh = q.shape
    outs, lses = [], []
    for window, dil in DILATED_PATTERNS:
        n = window // dil
        L = s_len // dil
        nb = -(-L // n)
        Lp = nb * n

        def gather(a):
            a = a.reshape(bsz, L, dil, nh, dh).swapaxes(1, 2)
            a = jnp.pad(a, ((0, 0), (0, 0), (0, Lp - L), (0, 0), (0, 0)))
            return a.reshape(bsz, dil, nb, n, nh, dh)

        def band(a):
            prev = jnp.pad(a, ((0, 0), (0, 0), (1, 0), (0, 0), (0, 0), (0, 0)))[:, :, :-1]
            return jnp.concatenate([prev, a], axis=3)

        qb = gather(q)
        kb = band(gather(k))
        vb = band(gather(v))
        s = jnp.einsum('brnqhd,brnkhd->brnhqk', qb, kb, preferred_element_type=F32) * dh ** -0.5
        kj = jnp.arange(2 * n)
        step = jnp.arange(n)[:, None] + n - kj[None, :]
        valid = ((step >= 0) & (step <= n))[None] & ((jnp.arange(nb)[:, None, None] > 0) | (kj >= n)[None, None, :])
        s = s - slopes[:, None, None] * (step * dil).astype(F32)
        s = jnp.where(valid[:, None], s, -jnp.inf)
        m = jnp.max(s, axis=-1, keepdims=True)
        p = jnp.exp(s - m)
        den = jnp.sum(p, axis=-1, keepdims=True)
        o = jnp.einsum('brnhqk,brnkhd->brnqhd', (p / den).astype(v.dtype), vb)
        lse = (m + jnp.log(den))[..., 0].swapaxes(-1, -2)

        def ungather(a):
            tr = a.shape[4:]
            a = a.reshape((bsz, dil, Lp) + tr)[:, :, :L]
            return a.swapaxes(1, 2).reshape((bsz, s_len) + tr)

        outs.append(ungather(o))
        lses.append(ungather(lse))
    w = jax.nn.softmax(jnp.stack(lses, axis=0), axis=0)
    out = jnp.sum(w[..., None] * jnp.stack(outs, axis=0).astype(F32), axis=0)
    return out.astype(q.dtype)

def sparse_attention(q, k, v, q_idx, k_idx, w_idx, slopes):
    s_len, dh = q.shape[1], q.shape[3]
    topk = min(TOPK_MAX, s_len // 4)
    nb = s_len // Q_BLOCK
    key_pos = jnp.arange(s_len)
    take = jax.vmap(lambda a, i: a[i])

    def block(args):
        qb, qib, wb, start = args
        qpos = start + jnp.arange(Q_BLOCK)
        logits = jnp.einsum('bqhd,bsd->bqhs', qib, k_idx, preferred_element_type=F32) * IDX_DIM ** -0.5
        score = jnp.einsum('bqh,bqhs->bqs', wb.astype(F32) * IDX_HEADS ** -0.5, jax.nn.relu(logits))
        score = jnp.where(key_pos[None, None, :] <= qpos[None, :, None], score, -jnp.inf)
        _, idx = lax.top_k(score, topk)
        valid = idx <= qpos[None, :, None]
        kg = take(k, idx)
        vg = take(v, idx)
        s = jnp.einsum('bqhd,bqkhd->bhqk', qb, kg, preferred_element_type=F32) * dh ** -0.5
        dist = (qpos[None, :, None] - idx).astype(F32)
        s = s - slopes[None, :, None, None] * dist[:, None]
        s = jnp.where(valid[:, None], s, -jnp.inf)
        p = jax.nn.softmax(s, axis=-1)
        return jnp.einsum('bhqk,bqkhd->bqhd', p.astype(v.dtype), vg)

    out = lax.map(block, (to_blocks(q), to_blocks(q_idx), to_blocks(w_idx), jnp.arange(nb) * Q_BLOCK))
    return from_blocks(out)

def second_inputs(seed: int = 0) -> dict:
    key = jax.random.key(seed)
    ks = jax.random.split(key, 14)
    nrm = jax.random.normal
    return {
        "x": nrm(ks[0], (BATCH, SEQ, D_MODEL), F32),
        "c": nrm(ks[1], (BATCH, D_MODEL), F32),
        "w_ada": nrm(ks[2], (DEPTH, D_MODEL, 3 * D_MODEL), F32) * (0.1 * D_MODEL ** -0.5),
        "b_ada": nrm(ks[3], (DEPTH, 3 * D_MODEL), F32) * 0.02,
        "w_in": nrm(ks[4], (DEPTH, D_MODEL, IN_WIDTH_2), F32) * D_MODEL ** -0.5,
        "q_norm_g": 1.0 + 0.02 * nrm(ks[5], (DEPTH, Q_LORA), F32),
        "kv_norm_g": 1.0 + 0.02 * nrm(ks[6], (DEPTH, KV_LORA), F32),
        "w_uq": nrm(ks[7], (DEPTH, Q_LORA, A_HEADS * (A_NOPE + A_ROPE)), F32) * Q_LORA ** -0.5,
        "w_uk": nrm(ks[8], (DEPTH, KV_LORA, A_HEADS * A_NOPE), F32) * KV_LORA ** -0.5,
        "w_uv": nrm(ks[9], (DEPTH, KV_LORA, A_HEADS * A_V), F32) * KV_LORA ** -0.5,
        "w_out": nrm(ks[10], (DEPTH, MIX_WIDTH_2, D_MODEL), F32) * (BETA * MIX_WIDTH_2 ** -0.5),
        "ln_g": 1.0 + 0.02 * nrm(ks[11], (DEPTH, D_MODEL), F32),
        "ln_b": 0.02 * nrm(ks[12], (DEPTH, D_MODEL), F32),
    }

def second_block(x, c, w_ada, b_ada, w_in, q_norm_g, kv_norm_g, w_uq, w_uk, w_uv, w_out, ln_g, ln_b):
    bsz, s_len, _ = x.shape
    slopes = alibi_slopes()
    slopes_b, slopes_c = slopes[:B_HEADS], slopes[B_HEADS:]
    pos = jnp.arange(s_len, dtype=F32)
    freqs = ROPE_THETA ** (-jnp.arange(0, A_ROPE, 2, dtype=F32) / A_ROPE)
    ang = pos[:, None] * freqs[None, :]
    cos, sin = jnp.cos(ang), jnp.sin(ang)

    def heads(a, n):
        return a.reshape(bsz, s_len, n, -1)

    for l in range(DEPTH):
        mod = jax.nn.silu(c) @ w_ada[l] + b_ada[l]
        shift, scale, gate = jnp.split(mod, 3, axis=-1)
        h = x * (1.0 + scale[:, None, :]) + shift[:, None, :]
        (p_cq, p_ckv, p_kr, p_qb, p_kb, p_vb, p_qc, p_kc, p_vc,
         p_qi, p_ki, p_wi, p_gate) = jnp.split(h @ w_in[l], SPLIT_POINTS, axis=-1)

        cq = rms_norm(p_cq, q_norm_g[l])
        ckv = rms_norm(p_ckv, kv_norm_g[l])
        qa = heads(cq @ w_uq[l], A_HEADS)
        qa_nope = qa[..., :A_NOPE]
        qa_rope = apply_rope_2(qa[..., A_NOPE:], cos[:, None, :], sin[:, None, :])
        ka_nope = heads(ckv @ w_uk[l], A_HEADS)
        va = heads(ckv @ w_uv[l], A_HEADS)
        ka_rope = apply_rope_2(p_kr, cos, sin)
        o_a = mla_attention(qa_nope, qa_rope, ka_nope, ka_rope, va)

        o_b = dilated_attention(heads(p_qb, B_HEADS), heads(p_kb, B_HEADS), heads(p_vb, B_HEADS), slopes_b)

        o_c = sparse_attention(heads(p_qc, C_HEADS), heads(p_kc, C_HEADS), heads(p_vc, C_HEADS),
                               heads(p_qi, IDX_HEADS), p_ki, p_wi, slopes_c)

        y = jnp.concatenate([o_a.reshape(bsz, s_len, A_WIDTH),
                             o_b.reshape(bsz, s_len, B_WIDTH),
                             o_c.reshape(bsz, s_len, C_WIDTH)], axis=-1) * jax.nn.silu(p_gate)
        sub = y @ w_out[l]
        x = layer_norm_2(ALPHA * x + (1.0 + gate[:, None, :]) * sub, ln_g[l], ln_b[l])
    return x


def setup_inputs(seed=0):
    out = dict(first_inputs(seed))
    for name, value in second_inputs(seed + 1).items():
        if name != "x":
            out[name + "_2"] = value
    return out


def reference(
    x, w_in, w_out, attn_sinks, ffn1_w_gu, ffn1_w_down, ffn2_w_gu, ffn2_w_down, ln1_g, ln1_b,
    ln2_g, ln2_b, ln3_g, ln3_b, c_2, w_ada_2, b_ada_2, w_in_2, q_norm_g_2, kv_norm_g_2, w_uq_2,
    w_uk_2, w_uv_2, w_out_2, ln_g_2, ln_b_2,
):
    x = first_block(
        x, w_in, w_out, attn_sinks, ffn1_w_gu, ffn1_w_down, ffn2_w_gu, ffn2_w_down, ln1_g,
        ln1_b, ln2_g, ln2_b, ln3_g, ln3_b,
    )
    return second_block(
        x, c_2, w_ada_2, b_ada_2, w_in_2, q_norm_g_2, kv_norm_g_2, w_uq_2, w_uk_2, w_uv_2,
        w_out_2, ln_g_2, ln_b_2,
    )


_drawn_inputs = setup_inputs


def setup_inputs(seed=0):
    import zlib

    import numpy as np

    out = dict(_drawn_inputs(seed))
    spreads = {}
    factors = {'attn_sinks': 8.0, 'b_ada_2': 5.918, 'q_norm_g_2': 8.0, 'kv_norm_g_2': 8.0}
    for name, (base, spread) in spreads.items():
        noise = np.random.default_rng([zlib.crc32(name.encode()), seed]).standard_normal(out[name].shape)
        drawn = base * np.exp(spread * noise) if base else spread * noise
        out[name] = __import__('jax').numpy.asarray(drawn.astype(out[name].dtype))
    for name, factor in factors.items():
        out[name] = (out[name] * factor).astype(out[name].dtype)
    return out
```

```python
import math
from contextlib import ExitStack

import numpy as np

import concourse.bass as bass
from concourse import mybir

F32 = mybir.dt.float32
F32R = mybir.dt.float32r
ALU = mybir.AluOpType
ACT = mybir.ActivationFunctionType
AX_X = mybir.AxisListType.X

P = 128
S = 256
TT = S // P
D = 1024
KT = D // P
HD = 64
DEPTH = 2
F = 2816
FU = 256
ROUNDS = F // FU
SLOTS = 3
UNIT = KT * FU
HALF = 512
ALPHA = (2 * DEPTH) ** 0.25
LN_EPS = 1e-5
GN_EPS = 1e-6
RMS_EPS = 1e-6
NEG = -1e30
TAKEN = -3e38
TOPK = min(256, S // 4)

ATTN1_HEADS, KV1_HEADS, RET_HEADS = 8, 2, 8
QA, KA, VA, QR, KR, VR, GR = 0, 512, 640, 768, 1280, 1792, 2304
IN1 = 2816
MIX1_COLS = [(c, 256) for c in range(0, 2560, 256)] + [(2560, 128), (2688, 128)]
MIX1_PROJ = len(MIX1_COLS)

A_HEADS, A_NOPE, A_ROPE, B_HEADS, C_HEADS, IDX_HEADS = 6, 64, 32, 6, 4, 8
A_HD = A_NOPE + A_ROPE
CQ, CKV, KROPE, QB, KB, VB, QC, KC, VC, QI, KI, WI, GATE = (
    0, 768, 1024, 1056, 1440, 1824, 2208, 2464, 2720, 2976, 3488, 3552, 3560)
Q_LORA, KV_LORA = 768, 256

R_CQ, R_CKV = 0, 768
R_QA, R_VA = 0, 576
R_VB, R_KR, R_WI = 1024, 1408, 1440
R_VC, R_GATE = 1448, 1704
R_ROW = 2728
C_QI, C_KI, C_QKB, C_QKC = 0, 4, 5, 11
C_TILES = 15

MIX2_UNITS = [
    ("T", [(QI, 256)], C_QI), ("T", [(QI + 256, 256)], C_QI + 2),
    ("T", [(KI, 64), (KI, 64)], C_KI),
    ("N", [(VB + 256, 128), (KROPE, 32), (WI, 8)], R_VB + 256),
    ("N", [(CQ, 256)], R_CQ), ("N", [(CQ + 256, 256)], R_CQ + 256), ("N", [(CQ + 512, 256)], R_CQ + 512),
    ("N", [(CKV, 256)], R_CKV),
    ("T", [(QB, 256)], C_QKB), ("T", [(QB + 256, 256)], C_QKB + 2), ("T", [(QB + 512, 256)], C_QKB + 4),
    ("N", [(VB, 256)], R_VB),
    ("UQ", 0), ("UQ", 1), ("UQ", 2), ("UK", 0), ("UK", 1), ("UV", 0), ("UV", 1),
    ("T", [(QC, 256)], C_QKC), ("T", [(QC + 256, 256)], C_QKC + 2),
    ("N", [(VC, 256)], R_VC),
    ("N", [(GATE, 256)], R_GATE), ("N", [(GATE + 256, 256)], R_GATE + 256),
    ("N", [(GATE + 512, 256)], R_GATE + 512), ("N", [(GATE + 768, 256)], R_GATE + 768),
]
MIX2_PROJ = len(MIX2_UNITS)
OUT_UNITS = 4
ADA_UNITS = 3 * D // FU

STEPS1 = [("W", 0, (0, 1, 2, 3)), ("W", 1, (0, 1)), ("W", 1, (2, 3))]
STEPS2 = {"B": [("B", 0, (0, 1, 2)), ("B", 1, (0, 1)), ("B", 1, (2,))],
          "A": [("A", 0, (0, 1, 2)), ("A", 1, (0, 1)), ("A", 1, (2,))],
          "C": [("C", 0, (0, 1)), ("C", 1, (0, 1))]}
IDX_STEPS = [(0, (0, 1, 2, 3)), (1, (0, 1)), (1, (2, 3))]

MIX1_WALK = (
    [("unit", 0), ("unit", 1), ("unit", 2), ("rope1",), ("unit", 3), ("trqk",),
     ("unit", 4), ("score", 0), ("unit", 5), ("score", 1), ("turn", 0),
     ("unit", 6), ("rotate",), ("score", 2), ("turn", 1), ("mix", 0), ("unit", 7), ("turn", 2), ("mix", 1),
     ("unit", 8), ("mix", 2), ("trret", 0), ("trret", 1),
     ("unit", 9), ("trret", 2), ("trret", 3), ("ret", 0), ("attn_out",), ("unit", 10),
     ("retmix", 0), ("ret", 1), ("unit", 11), ("retmix", 1), ("ret", 2),
     ("ycols", 0, 0), ("ycols", 1, 0), ("retmix", 2), ("ret", 3), ("retmix", 3),
     ("groupnorm",), ("out", 0), ("out", 1), ("ycols", 0, 1), ("ycols", 1, 1), ("out", 2), ("out", 3)])

MIX2_WALK = (
    [("unit", 0), ("unit", 1), ("unit", 2), ("unit", 3), ("idxw",),
     ("unit", 4), ("idx", 0), ("unit", 5), ("idx", 1), ("unit", 6), ("idx", 2), ("unit", 7), ("latent",),
     ("topk", 0), ("unit", 8), ("trlat", 0), ("trlat", 1), ("unit", 9), ("topk", 1),
     ("trlat", 2), ("trlat", 3), ("unit", 10), ("unit", 11), ("score", "B", 0),
     ("unit", 12), ("score", "B", 1), ("turn", "B", 0), ("unit", 13), ("score", "B", 2), ("turn", "B", 1),
     ("mix", "B", 0), ("unit", 14), ("turn", "B", 2), ("mix", "B", 1), ("unit", 15), ("mix", "B", 2),
     ("unit", 16), ("unit", 17), ("ropeA",), ("unit", 18), ("unit", 19), ("trA", 0), ("trA", 1), ("trA", 2),
     ("unit", 20), ("trA", 3), ("trA", 4), ("trA", 5), ("score", "A", 0),
     ("unit", 21), ("score", "A", 1), ("turn", "A", 0), ("unit", 22), ("score", "A", 2),
     ("turn", "A", 1), ("mix", "A", 0), ("unit", 23), ("turn", "A", 2), ("mix", "A", 1), ("score", "C", 0),
     ("unit", 24), ("mix", "A", 2), ("score", "C", 1), ("turn", "C", 0), ("unit", 25), ("turn", "C", 1),
     ("mix", "C", 0), ("gates",), ("mix", "C", 1),
     ("ycols", 0, 0), ("ycols", 1, 0), ("ycols", 0, 1), ("ycols", 1, 1),
     ("out", 0), ("out", 1), ("out", 2), ("ycols", 0, 2), ("ycols", 1, 2), ("out", 3)])
YPARTS1 = [(0, 1, 2, 3), (4, 5, 6, 7)]
YPARTS2 = [(0, 1, 2), (3, 4, 5), (6, 7)]


def ps_turns(walk):
    turns, n = {}, [0, 0]
    for job in walk:
        banks = {"turn": (0, 1), "trqk": (0, 1, 0), "trlat": (0,), "trA": (0,), "trret": (0,),
                 "ycols": (0,)}.get(job[0], ())
        if job[0] in ("trlat", "trA", "trret"):
            banks = (job[1] % 2,)
        if job[0] == "ycols":
            banks = (job[1],)
        got = []
        for b in banks:
            got.append((b, n[b]))
            n[b] += 1
        if got:
            turns[job] = got
    return turns, n


TURNS1, NTURNS1 = ps_turns(MIX1_WALK)
TURNS2, NTURNS2 = ps_turns(MIX2_WALK)

STAGES1 = ["ffn", "norm", "mix1", "norm", "ffn", "norm"]
STAGES2 = ["ada", "mix2", "norm"]
SIGNALS = {
    "ffn": dict(turned0=TT, turned1=TT, free0=TT, free1=TT, hi_part=2 * TT, silu_done=ROUNDS, h_done=ROUNDS,
                h_hi=ROUNDS, h_lo=ROUNDS, sum_ready=TT),
    "norm": dict(var_ready=TT, rstd_ready=TT, x_ready=TT),
    "mix1": dict(turned0=TT + NTURNS1[0], turned1=TT + NTURNS1[1], free0=TT + NTURNS1[0],
                 free1=TT + NTURNS1[1], hi_part=2 * TT + 4, proj_copied=MIX1_PROJ, rope_done=1, rotated=1,
                 scores=2 * 7, score_free=2 * 7, maxed=3, probs=3, mixed=3, ret_mixed=4, y_ready=4,
                 var_ready=TT, rstd_ready=TT, out_copied=TT, sink_sum=1, sink_exp=1, sum_ready=TT),
    "ada": dict(c_hi=1, c_lo=1, mod_ready=ADA_UNITS, h_ready=TT),
    "mix2": dict(turned0=TT + NTURNS2[0], turned1=TT + NTURNS2[1], free0=TT + NTURNS2[0],
                 free1=TT + NTURNS2[1], hi_part=2 * TT + 4 + 6, proj_copied=MIX2_PROJ, rope_done=1,
                 scores=2 * 11, score_free=2 * 11, idx_summed=3, maxed=8, probs=8, mixed=8, out_copied=6,
                 squares=1, var_ready=1, rstd_ready=1, latent=TT, gates=1, y_ready=6, sum_ready=TT),
}
NAMES = sorted({n for s in SIGNALS.values() for n in s})
RING_USES = {"mix1": MIX1_PROJ + OUT_UNITS, "ada": ADA_UNITS, "mix2": MIX2_PROJ + OUT_UNITS}


def signals_before(block, layer, position, name):
    total = lambda stages: sum(SIGNALS[s].get(name, 0) for s in stages)
    if block == 1:
        return layer * total(STAGES1) + total(STAGES1[:position])
    return DEPTH * total(STAGES1) + layer * total(STAGES2) + total(STAGES2[:position])


def slot_uses(stage, first):
    n = [0] * SLOTS
    if stage == "ffn":
        n[first] += ROUNDS + 1
        n[(first + 1) % SLOTS] += ROUNDS
        n[(first + 2) % SLOTS] += ROUNDS - 1
        return n, (first + 1) % SLOTS
    units = RING_USES.get(stage, 0)
    for m in range(units):
        n[(first + m) % SLOTS] += 1
    return n, (first + units) % SLOTS


def ring_plan(stages):
    plan, first, seen = [], 0, [0] * SLOTS
    for stage in stages:
        plan.append((first, list(seen)))
        uses, first = slot_uses(stage, first)
        seen = [a + b for a, b in zip(seen, uses)]
    assert first == 0, "a layer has to end where the next one begins"
    return plan, seen


RING1, LAYER_USES1 = ring_plan(STAGES1)
RING2, LAYER_USES2 = ring_plan(STAGES2)


class Stage:

    def __init__(self, block, layer, position):
        self.block, self.layer, self.position = block, layer, position
        self.first, self.seen = (RING1 if block == 1 else RING2)[position]

    def before(self, name):
        return signals_before(self.block, self.layer, self.position, name)

    def uses(self, slot):
        if self.block == 1:
            return self.layer * LAYER_USES1[slot] + self.seen[slot]
        return DEPTH * LAYER_USES1[slot] + self.layer * LAYER_USES2[slot] + self.seen[slot]

    def unit(self, m):
        slot = (self.first + m) % SLOTS
        return slot, self.uses(slot) + m // SLOTS


class Steps:

    def __init__(self, eng, sem, marks):
        self.eng, self.sem, self.marks, self.base, self.n = eng, sem, marks, 0, 0

    def wait(self, instruction):
        instruction.then_inc(self.sem, 1)
        self.n += 1
        self.eng.wait_ge(self.sem, self.base + self.n)

    def settle(self):
        self.eng.sem_inc(self.marks, 1)

    def loop(self, first, last, name):
        reg = self.eng.alloc_register(name)
        self.settle()
        self.eng.reg_mov(reg, self.eng.compute_val(self.base + self.n) if not isinstance(self.base, int)
                         else self.base + self.n)
        return _Loop(self, first, last, reg)


class _Loop:
    def __init__(self, steps, first, last, reg):
        self.steps, self.first, self.last, self.reg = steps, first, last, reg

    def __enter__(self):
        s = self.steps
        self.outer = (s.base, s.n)
        self.fori = s.eng.Fori(self.first, self.last)
        i = self.fori.__enter__()
        s.base, s.n = s.eng.snap(self.reg), 0
        return i

    def __exit__(self, *a):
        s = self.steps
        s.settle()
        s.eng.reg_add(self.reg, self.reg, s.n)
        self.fori.__exit__(*a)
        s.base, s.n = self.outer[0], self.outer[1] + (self.last - self.first) * s.n
        return False


T1_MASK, T1_DECAY, T1_ROPE, T1_RET = 0, 256, 256 + 2048, 256 + 2048 + 128
T1 = T1_RET + 128
T2_MASK, T2_B, T2_C, T2_ROPE = 0, 256, 256 + 6 * 256, 256 + 10 * 256
T2 = T2_ROPE + 64


def shape_tables():
    row, col = np.arange(P)[:, None], np.arange(2 * P)[None, :]
    back = row + P - col
    tab1, tab2 = np.zeros((P, T1), np.float64), np.zeros((P, T2), np.float64)
    tab1[:, T1_MASK:T1_DECAY] = np.where((back >= 0) & (back < P), 0.0, NEG)
    log_gamma = np.log1p(-np.exp2(-5.0 - np.arange(RET_HEADS)))
    for h in range(RET_HEADS):
        at = T1_DECAY + (h % 2 * 4 + h // 2) * 256
        tab1[:, at:at + 256] = np.where(col >= row, np.exp((col - row) * log_gamma[h]), 0.0) * HD ** -0.5
    pos = np.arange(S, dtype=np.float64)[:, None]

    def rotation(freqs):
        ang = (pos.astype(np.float32) * freqs.astype(np.float32)[None, :]).astype(np.float64)
        both = np.concatenate([np.cos(ang), np.sin(ang)], axis=1)
        return both.reshape(TT, P, -1).transpose(1, 0, 2).reshape(P, -1)

    tab1[:, T1_ROPE:T1_RET] = rotation(10000.0 ** (-np.arange(0, HD, 2) / HD))
    tab1[:, T1_RET:T1] = rotation(1.0 / (10000.0 ** np.linspace(0.0, 1.0, HD // 2)))
    tab2[:, T2_MASK:T2_B] = np.where(back >= 0, 0.0, NEG)
    slopes = 2.0 ** (-8.0 * np.arange(1, B_HEADS + C_HEADS + 1) / (B_HEADS + C_HEADS))
    times = ((back >= 0) & (back <= P)).astype(int) + ((back >= 0) & (back % 4 == 0)) + ((back >= 0) & (back % 16 == 0))
    log_times = np.where(times > 0, np.log(np.maximum(times, 1)), NEG)
    for h in range(B_HEADS):
        at = T2_B + (h % 2 * 3 + h // 2) * 256
        tab2[:, at:at + 256] = np.where(times > 0, log_times - slopes[h] * back, NEG)
    for h in range(C_HEADS):
        at = T2_C + (h % 2 * 2 + h // 2) * 256
        tab2[:, at:at + 256] = np.where(back >= 0, -slopes[B_HEADS + h] * back, NEG)
    tab2[:, T2_ROPE:T2] = rotation(10000.0 ** (-np.arange(0, A_ROPE, 2) / A_ROPE))
    return tab1.astype(np.float32), tab2.astype(np.float32), np.eye(P, dtype=np.float32)


def head_of(group, pair, half):
    return pair + 4 * half if group == "W" else 2 * pair + half


def build(nc, t, out):
    with ExitStack() as ctx:
        def sb(name, shape, dt=F32):
            return ctx.enter_context(nc.sbuf_tensor(name, shape, dt))

        def sem(name):
            return ctx.enter_context(nc.semaphore(name))

        raw = [sb(f"w_raw{j}", [P, UNIT]) for j in range(SLOTS)]
        w_hi = [sb(f"w_hi{j}", [P, UNIT], F32R) for j in range(SLOTS)]
        w_lo = [sb(f"w_lo{j}", [P, UNIT], F32R) for j in range(SLOTS)]
        x = sb("x", [P, TT, D])
        y = sb("y", [P, TT, D])
        col_hi = sb("col_hi", [P, KT, S], F32R)
        col_lo = sb("col_lo", [P, KT, S], F32R)
        lat_hi = sb("lat_hi", [P, KT, S], F32R)
        lat_lo = sb("lat_lo", [P, KT, S], F32R)
        arena = sb("arena", [P, 10880])
        score = sb("score", [P, 2, HALF])
        prob = sb("prob", [P, 2, HALF])
        prob_t = sb("prob_t", [P, 2, HALF])
        table = sb("table", [P, max(T1, T2)])
        ident = sb("ident", [P, P])
        norm_g = sb("norm_g", [P, D])
        norm_b = sb("norm_b", [P, D])
        mod = sb("mod", [P, 3 * D])
        small = sb("small", [P, 320])

        silu_a, hidden = arena[:, 0:HALF], arena[:, HALF:2 * HALF]
        rows1 = arena[:, 0:TT * IN1].rearrange("p (t n) -> p t n", t=TT)
        o = TT * IN1
        q1_t = arena[:, o:o + 1024].rearrange("p (j s) -> p j s", j=4)
        k1_t = arena[:, o + 1024:o + 1280]
        qr_t = arena[:, o + 1280:o + 2304].rearrange("p (j s) -> p j s", j=4)
        kr_t = arena[:, o + 2304:o + 3328].rearrange("p (j s) -> p j s", j=4)
        rot_tmp = arena[:, o + 3328:o + 4352]
        rows2 = arena[:, 0:TT * R_ROW].rearrange("p (t n) -> p t n", t=TT)
        o = TT * R_ROW
        cols2 = arena[:, o:o + C_TILES * S].rearrange("p (j s) -> p j s", j=C_TILES)
        ka = arena[:, o:o + TT * A_HEADS * A_HD].rearrange("p (t h d) -> p t h d", t=TT, h=A_HEADS)
        qa_t = arena[:, o + C_QKB * S:o + C_QKC * S].rearrange("p (h s) -> p h s", h=A_HEADS)
        ka_t = mod[:, 0:A_HEADS * S].rearrange("p (h s) -> p h s", h=A_HEADS)
        o += C_TILES * S
        idx_score = arena[:, o:o + 512].rearrange("p (t s) -> p t s", t=TT)
        not_taken = arena[:, o + 512:o + 1024].rearrange("p (t s) -> p t s", t=TT)
        rope_tmp = arena[:, o + 1024:o + 1536]
        c_hi = lat_hi[:, 0:4, :].rearrange("p a b -> p (a b)").rearrange("p (k m) -> p k m", k=KT)
        c_lo = lat_lo[:, 0:4, :].rearrange("p a b -> p (a b)").rearrange("p (k m) -> p k m", k=KT)

        at = [0]

        def few(n):
            at[0] += n
            return small[:, at[0] - n:at[0]]
        stats = few(TT * 12).rearrange("p (t a b) -> p t a b", t=TT, a=2)
        mean_var = few(TT * 2).rearrange("p (t a) -> p t a", t=TT)
        rstd = few(TT)
        gn_sum = few(TT * 8).rearrange("p (t h) -> p t h", t=TT)
        gn_var = few(TT * 8).rearrange("p (t h) -> p t h", t=TT)
        gn_rstd = few(TT * 8).rearrange("p (t h) -> p t h", t=TT)
        lat_var = few(TT * 2).rearrange("p (a t) -> p a t", a=2)
        lat_rstd = few(TT * 2).rearrange("p (a t) -> p a t", a=2)
        row_max = few(TT * 8).rearrange("p (t h) -> p t h", t=TT)
        neg_max = few(TT * 8).rearrange("p (t h) -> p t h", t=TT)
        row_sum = few(TT * 8).rearrange("p (t h) -> p t h", t=TT)
        row_inv = few(TT * 8).rearrange("p (t h) -> p t h", t=TT)
        sink_e = few(TT * 8).rearrange("p (t h) -> p t h", t=TT)
        sinks = few(8)
        top8 = few(8)
        idx_w = few(TT * 8).rearrange("p (t h) -> p t h", t=TT)
        c_raw = few(KT)
        c_silu = few(KT)
        minus_half = few(8)

        ps = ctx.enter_context(nc.psum_tensor("ps", [P, 8, HALF], F32))

        landed = [sem(f"w_landed{j}") for j in range(SLOTS)]
        hi_ready = [sem(f"w_hi_ready{j}") for j in range(SLOTS)]
        lo_ready = [sem(f"w_lo_ready{j}") for j in range(SLOTS)]
        used = [sem(f"w_used{j}") for j in range(SLOTS)]
        k_piece, w_piece = sem("k_piece_landed"), sem("w_piece_landed")
        sg = {n: sem(n) for n in NAMES}
        x_landed, tables_in, ident_in = sem("x_landed"), sem("tables_landed"), sem("ident_landed")
        params_in, sinks_in, lat_g_in, mod_in, c_in = (
            sem("norm_params_landed"), sem("sinks_landed"), sem("latent_gains_landed"),
            sem("mod_bias_landed"), sem("c_landed"))
        const_ready, c_ready, out_landed = sem("const_ready"), sem("c_ready"), sem("out_landed")
        v_steps, a_steps, g_steps, p_marks, s_marks, a_marks, v_marks, t_marks = (
            sem(n) for n in ("vector_steps", "scalar_steps", "gpsimd_steps", "gpsimd_marks", "sync_marks",
                             "scalar_marks", "vector_marks", "tensor_marks"))
        turned, free = [sg["turned0"], sg["turned1"]], [sg["free0"], sg["free1"]]
        free_name = ["free0", "free1"]

        def bank(b, n=HALF):
            return ps[:, b, 0:n]

        def by_pair(tile, t_, group, pairs):
            if group == "W":
                v = tile[:, t_, :].rearrange("p (f j) -> p f j", f=2)
            else:
                v = tile[:, t_, :].rearrange("p (j f) -> p f j", f=2)
            return v[:, :, pairs[0]:pairs[-1] + 1]

        def group_heads(group):
            return {"W": 8, "A": 6, "B": 6, "C": 4}[group]

        steps_of = lambda group: STEPS1 if group == "W" else STEPS2[group]
        ORDER2 = {("B", 0): 0, ("B", 1): 1, ("B", 2): 2, ("A", 0): 3, ("A", 1): 4, ("A", 2): 5,
                  ("C", 0): 6, ("C", 1): 7}

        def ordinal(group, s):
            return s if group == "W" else ORDER2[group, s]

        def scored_before(group, s):
            return s if group == "W" else 3 + ORDER2[group, s]

        block = ctx.enter_context(nc.Block())

        @block.sync
        def _(sp):
            def settle():
                sp.sem_inc(s_marks, 1)

            def load(slot, use, dst, src, extra=()):
                sp.wait_ge(hi_ready[slot], use + 1)
                settle()
                sp.wait_ge(lo_ready[slot], use + 1)
                settle()
                sp.dma_start(dst, src).then_inc(landed[slot], 16)
                for d, s_, signal in extra:
                    sp.dma_start(d, s_).then_inc(signal, 16)

            def rows_of(slot, k, n):
                return raw[slot][:, 0:k * n].rearrange("p (k n) -> p k n", k=k)

            def ffn(st, l, gate_up, down):
                g, u, d = st.first, (st.first + 1) % SLOTS, (st.first + 2) % SLOTS
                def gu(i, slot, first_col):
                    load(slot, st.uses(slot) + i, rows_of(slot, KT, FU),
                         gate_up[l, :, bass.ds(first_col + i * FU, FU)].rearrange("(k p) n -> p k n", p=P))

                def dn(i, slot, use):
                    load(slot, use, rows_of(slot, 2, D),
                         down[l, bass.ds(i * FU, FU), :].rearrange("(k p) n -> p k n", p=P))
                for i in range(2):
                    gu(i, g, 0)
                    gu(i, u, F)
                with sp.Fori(1, ROUNDS - 1) as i:
                    dn(i - 1, d, st.uses(d) + i - 1)
                    gu(i + 1, g, 0)
                    gu(i + 1, u, F)
                dn(ROUNDS - 2, d, st.uses(d) + ROUNDS - 2)
                dn(ROUNDS - 1, g, st.uses(g) + ROUNDS)

            def out_units(st, l, first, w):
                for i in range(OUT_UNITS):
                    slot, use = st.unit(first + i)
                    load(slot, use, rows_of(slot, 2, D),
                         w[l, i * 2 * P:(i + 1) * 2 * P, :].rearrange("(k p) n -> p k n", p=P))

            with sp.Fori(0, DEPTH) as l:
                for pos, name in enumerate(STAGES1):
                    st = Stage(1, l, pos)
                    if name == "ffn":
                        n = 1 if pos == 0 else 2
                        ffn(st, l, t[f"ffn{n}_w_gu"], t[f"ffn{n}_w_down"])
                    if name == "mix1":
                        for m, (c, w) in enumerate(MIX1_COLS):
                            slot, use = st.unit(m)
                            load(slot, use, rows_of(slot, KT, w),
                                 t["w_in"][l, :, c:c + w].rearrange("(k p) n -> p k n", p=P))
                        out_units(st, l, MIX1_PROJ, t["w_out"])
            with sp.Fori(0, DEPTH) as l:
                st = Stage(2, l, 0)
                for m in range(ADA_UNITS):
                    slot, use = st.unit(m)
                    load(slot, use, rows_of(slot, KT, FU),
                         t["w_ada_2"][l, :, m * FU:(m + 1) * FU].rearrange("(k p) n -> p k n", p=P))
                st = Stage(2, l, 1)
                for m, unit in enumerate(MIX2_UNITS):
                    slot, use = st.unit(m)
                    if unit[0] in ("T", "N"):
                        width = sum(w for _, w in unit[1])
                        dst, c0, parts = rows_of(slot, KT, width), 0, []
                        for c, w in unit[1]:
                            parts.append((dst[:, :, c0:c0 + w],
                                          t["w_in_2"][l, :, c:c + w].rearrange("(k p) n -> p k n", p=P)))
                            c0 += w
                        signal = k_piece if unit[1][0][0] == KI else w_piece
                        load(slot, use, *parts[0], extra=[(d, s_, signal) for d, s_ in parts[1:]])
                    else:
                        w = {"UQ": t["w_uq_2"], "UK": t["w_uk_2"], "UV": t["w_uv_2"]}[unit[0]]
                        k = (Q_LORA if unit[0] == "UQ" else KV_LORA) // P
                        load(slot, use, rows_of(slot, k, 192),
                             w[l, :, unit[1] * 192:(unit[1] + 1) * 192].rearrange("(k p) n -> p k n", p=P))
                out_units(st, l, MIX2_PROJ, t["w_out_2"])
            sp.wait_ge(sg["x_ready"], TT + signals_before(2, DEPTH, 0, "x_ready"))
            sp.dma_start(out[0].rearrange("(t p) d -> p t d", p=P), x[:, :, :]).then_inc(out_landed, 16)
            sp.wait_ge(out_landed, 16)

        @block.tensor
        def _(pe):
            def unit_ready(slot, use):
                pe.wait_ge(hi_ready[slot], use + 2)
                pe.wait_ge(lo_ready[slot], use + 2)

            def three(dst, a_hi, a_lo, b_hi, b_lo, start, stop):
                pe.matmul(dst, a_hi, b_hi, start=start, stop=False)
                pe.matmul(dst, a_hi, b_lo, start=False, stop=False)
                return pe.matmul(dst, a_lo, b_hi, start=False, stop=stop)

            def turned_unit(slot, b, width, kt=KT):
                hi = w_hi[slot][:, 0:kt * width].rearrange("p (k n) -> p k n", k=kt)
                lo = w_lo[slot][:, 0:kt * width].rearrange("p (k n) -> p k n", k=kt)
                for n in range(width // P):
                    for k in range(kt):
                        last = three(ps[:, b, n * S:(n + 1) * S], hi[:, k, n * P:(n + 1) * P],
                                     lo[:, k, n * P:(n + 1) * P], col_hi[:, k, :], col_lo[:, k, :],
                                     k == 0, k == kt - 1)
                last.then_inc(used[slot], 1)

            def row_unit(slot, b, width, a_hi, a_lo, kts, tiles=TT, step=P):
                hi = w_hi[slot][:, 0:len(kts) * width].rearrange("p (k n) -> p k n", k=len(kts))
                lo = w_lo[slot][:, 0:len(kts) * width].rearrange("p (k n) -> p k n", k=len(kts))
                for i in range(tiles):
                    tok = slice(i * step, i * step + P)
                    for k, kk in enumerate(kts):
                        last = three(ps[:, b, i * 256:i * 256 + width], a_hi[:, kk, tok], a_lo[:, kk, tok],
                                     hi[:, k, :], lo[:, k, :], k == 0, k == len(kts) - 1)
                last.then_inc(used[slot], 1)

            def wide_unit(slot, banks, a_hi, a_lo, kts, start, stop, signal=None):
                hi = w_hi[slot][:, :].rearrange("p (k n) -> p k n", k=2)
                lo = w_lo[slot][:, :].rearrange("p (k n) -> p k n", k=2)
                for i in range(TT):
                    for n in range(2):
                        for k, kk in enumerate(kts):
                            cols = slice(n * HALF, (n + 1) * HALF)
                            last = three(bank(banks[i] + n), a_hi[:, kk, i * P:(i + 1) * P],
                                         a_lo[:, kk, i * P:(i + 1) * P], hi[:, k, cols], lo[:, k, cols],
                                         start and k == 0, stop and k == 1)
                    if signal is not None and i < TT - 1:
                        last.then_inc(signal, 1)
                return last

            def turn_rows(st, src, wait_name, wait_base):
                for i in range(TT):
                    pe.wait_ge(sg[wait_name], wait_base + i + 1)
                    for hf in range(2):
                        pe.wait_ge(free[hf], st.before(free_name[hf]) + i + 1)
                        for k in range(4):
                            last = pe.transpose(ps[:, 6 + hf, k * P:(k + 1) * P],
                                                src[:, i, (4 * hf + k) * P:(4 * hf + k + 1) * P], ident[:, :])
                        last.then_inc(turned[hf], 1)
                for hf in range(2):
                    pe.wait_ge(free[hf], st.before(free_name[hf]) + TT + 1)

            def ffn(st):
                g, u, d = st.first, (st.first + 1) % SLOTS, (st.first + 2) % SLOTS
                turn_rows(st, x, "x_ready", st.before("x_ready"))
                h_hi = lambda s_: lat_hi[:, 2 * s_:2 * s_ + 2, :]
                h_lo = lambda s_: lat_lo[:, 2 * s_:2 * s_ + 2, :]

                def gate(i):
                    unit_ready(g, st.uses(g) + i)
                    turned_unit(g, 4, FU)

                def up(i):
                    unit_ready(u, st.uses(u) + i)
                    turned_unit(u, 5, FU)

                def down(i, slot, use, s_, start=False, stop=False):
                    unit_ready(slot, use)
                    pe.wait_ge(sg["h_lo"], st.before("h_lo") + i + 1)
                    last = wide_unit(slot, (0, 2), h_hi(s_), h_lo(s_), (0, 1), start, stop,
                                     sg["sum_ready"] if stop else None)
                    if not stop:
                        last.then_inc(used[slot], 1)
                    else:
                        last.then_inc(sg["sum_ready"], 1)
                        pe.sem_inc(used[slot], 1)

                gate(0)
                up(0)
                for i in (1,):
                    pe.wait_ge(sg["silu_done"], st.before("silu_done") + i)
                    gate(i)
                    pe.wait_ge(sg["h_done"], st.before("h_done") + i)
                    up(i)
                    down(0, d, st.uses(d), 0, start=True)
                with pe.Fori(2, ROUNDS - 1) as i:
                    pe.wait_ge(sg["silu_done"], st.before("silu_done") + i)
                    gate(i)
                    pe.wait_ge(sg["h_done"], st.before("h_done") + i)
                    up(i)
                    down(i - 1, d, st.uses(d) + i - 1, 0)
                i = ROUNDS - 1
                pe.wait_ge(sg["silu_done"], st.before("silu_done") + i)
                gate(i)
                pe.wait_ge(sg["h_done"], st.before("h_done") + i)
                up(i)
                down(i - 1, d, st.uses(d) + i - 1, 0)
                down(i, g, st.uses(g) + ROUNDS, 1, stop=True)

            def turn_banks(st, turns, job, tiles, which=0):
                b, n = turns[job][which]
                pe.wait_ge(free[b], st.before(free_name[b]) + TT + n + 1)
                for src, c in tiles:
                    width = math.prod(src.shape[1:])
                    last = pe.transpose(ps[0:width, 6 + b, c:c + P], src, ident[:, :])
                last.then_inc(turned[b], 1)

            def scores_free(st, before):
                if before:
                    pe.wait_ge(sg["score_free"], st.before("score_free") + 2 * before)

            def attend_scores(st, group, s):
                _, i, pairs = steps_of(group)[s]
                scores_free(st, scored_before(group, s))
                keys = (i + 1) * P
                for half in range(2):
                    for n, j in enumerate(pairs):
                        rows = slice(64 * half, 64 * half + 64)
                        toks = slice(i * P, (i + 1) * P)
                        if group == "W":
                            q, k = q1_t[rows, j, toks], k1_t[rows, 0:keys]
                        elif group == "B":
                            q, k = cols2[rows, C_QKB + j, toks], cols2[rows, C_QKB + 3 + j, 0:keys]
                        elif group == "C":
                            q, k = cols2[rows, C_QKC + j, toks], cols2[rows, C_QKC + 2 + j, 0:keys]
                        else:
                            q, k = qa_t[0:A_HD, 2 * j + half, toks], ka_t[0:A_HD, 2 * j + half, 0:keys]
                        last = pe.matmul(ps[:, half, n * keys:(n + 1) * keys], q, k, start=True, stop=True)
                    last.then_inc(sg["scores"], 1)

            def attend_turn(st, turns, group, s):
                job = ("turn", s) if group == "W" else ("turn", group, s)
                _, i, pairs = steps_of(group)[s]
                pe.wait_ge(sg["probs"], st.before("probs") + ordinal(group, s) + 1)
                for half in range(2):
                    n = len(pairs) * (i + 1)
                    turn_banks(st, turns, job, [(prob[:, half, c * P:(c + 1) * P], c * P) for c in range(n)], half)

            def attend_mix(st, turns, group, s):
                job = ("turn", s) if group == "W" else ("turn", group, s)
                _, i, pairs = steps_of(group)[s]
                for half in range(2):
                    b, n = turns[job][half]
                    pe.wait_ge(free[b], st.before(free_name[b]) + TT + n + 2)
                if group in "AC" and s == 0:
                    pe.wait_ge(sg["out_copied"], st.before("out_copied") + (2 if group == "A" else 4))
                for half in range(2):
                    for n, j in enumerate(pairs):
                        h = head_of(group, j, half)
                        for k in range(i + 1):
                            v = {"W": rows1[:, k, VA + half * HD:VA + half * HD + HD] if group == "W" else None,
                                 "A": rows2[:, k, R_VA + h * HD:R_VA + h * HD + HD],
                                 "B": rows2[:, k, R_VB + h * HD:R_VB + h * HD + HD],
                                 "C": rows2[:, k, R_VC + h % 4 * HD:R_VC + h % 4 * HD + HD]}[group]
                            c = (n * (i + 1) + k) * P
                            last = pe.matmul(ps[:, 2 + i, h * HD:(h + 1) * HD], prob_t[:, half, c:c + P], v,
                                             start=k == 0, stop=k == i)
                last.then_inc(sg["mixed"], 1)

            def y_turn(st, turns, job, parts):
                _, i, part = job
                order = [j for j in (MIX1_WALK if st.block == 1 else MIX2_WALK) if j[0] == "ycols"].index(job)
                pe.wait_ge(sg["y_ready"], st.before("y_ready") + order + 1)
                turn_banks(st, turns, job, [(y[:, i, k * P:(k + 1) * P], n * P)
                                            for n, k in enumerate(parts[part])])

            def out_unit(st, turns, i, first, parts, scored):
                slot, use = st.unit(first + i)
                unit_ready(slot, use)
                if i == 0:
                    scores_free(st, scored)
                    pe.wait_ge(sg["proj_copied"], st.before("proj_copied") + first)
                kts = (2 * i, 2 * i + 1)
                for part, tiles in enumerate(parts):
                    if set(kts) & set(tiles):
                        for tok in range(TT):
                            b, n = turns["ycols", tok, part][0]
                            pe.wait_ge(free[b], st.before(free_name[b]) + TT + n + 2)
                final = i == OUT_UNITS - 1
                last = wide_unit(slot, (0, 4), col_hi, col_lo, kts, i == 0, final,
                                 sg["sum_ready"] if final else None)
                if final:
                    last.then_inc(sg["sum_ready"], 1)
                    pe.sem_inc(used[slot], 1)
                else:
                    last.then_inc(used[slot], 1)

            def mix1(st):
                turn_rows(st, x, "x_ready", st.before("x_ready"))
                for job in MIX1_WALK:
                    if job[0] == "unit":
                        m = job[1]
                        slot, use = st.unit(m)
                        unit_ready(slot, use)
                        if m >= 2:
                            pe.wait_ge(sg["proj_copied"], st.before("proj_copied") + m - 1)
                        row_unit(slot, 4 + m % 2, MIX1_COLS[m][1], col_hi, col_lo, range(KT))
                    elif job[0] == "trqk":
                        pe.wait_ge(sg["rope_done"], st.before("rope_done") + 1)
                        for i in range(TT):
                            turn_banks(st, TURNS1, job, [(rows1[:, i, QA + j * P:QA + (j + 1) * P], j * P)
                                                         for j in range(4)], i)
                        turn_banks(st, TURNS1, job, [(rows1[:, i, KA:VA], i * P) for i in range(TT)], 2)
                    elif job[0] == "score":
                        if job[1] == 0:
                            for which in range(3):
                                b, n = TURNS1["trqk",][which]
                                pe.wait_ge(free[b], st.before(free_name[b]) + TT + n + 2)
                        attend_scores(st, "W", job[1])
                    elif job[0] == "turn":
                        attend_turn(st, TURNS1, "W", job[1])
                    elif job[0] == "mix":
                        attend_mix(st, TURNS1, "W", job[1])
                    elif job[0] == "trret":
                        if job[1] == 0:
                            pe.wait_ge(sg["rotated"], st.before("rotated") + 1)
                        c, i = (QR, KR)[job[1] // 2], job[1] % 2
                        turn_banks(st, TURNS1, job, [(rows1[:, i, c + j * P:c + (j + 1) * P], j * P) for j in range(4)])
                    elif job[0] == "ret":
                        j = job[1]
                        if j == 0:
                            for b in range(2):
                                n = TURNS1["trret", 2 + b][0][1]
                                pe.wait_ge(free[b], st.before(free_name[b]) + TT + n + 2)
                        scores_free(st, 3 + j)
                        for half in range(2):
                            rows = slice(64 * half, 64 * half + 64)
                            pe.matmul(ps[:, half, 0:S], kr_t[rows, j, 0:P], qr_t[rows, j, :], start=True, stop=True)
                            pe.matmul(ps[:, half, S:S + P], kr_t[rows, j, P:S], qr_t[rows, j, P:S],
                                      start=True, stop=True).then_inc(sg["scores"], 1)
                    elif job[0] == "retmix":
                        j = job[1]
                        if j == 0:
                            pe.wait_ge(sg["out_copied"], st.before("out_copied") + TT)
                        pe.wait_ge(sg["score_free"], st.before("score_free") + 2 * (4 + j))
                        decayed = prob if j % 2 == 0 else score
                        for half in range(2):
                            h = 2 * j + half
                            v = lambda k: rows1[:, k, VR + h * HD:VR + (h + 1) * HD]
                            o_ = slice(h * HD, (h + 1) * HD)
                            pe.matmul(ps[:, 2, o_], decayed[:, half, 0:P], v(0), start=True, stop=True)
                            pe.matmul(ps[:, 3, o_], decayed[:, half, P:S], v(0), start=True, stop=False)
                            last = pe.matmul(ps[:, 3, o_], decayed[:, half, S:S + P], v(1), start=False, stop=True)
                        last.then_inc(sg["ret_mixed"], 1)
                    elif job[0] == "ycols":
                        y_turn(st, TURNS1, job, YPARTS1)
                    elif job[0] == "out":
                        out_unit(st, TURNS1, job[1], MIX1_PROJ, YPARTS1, 7)

            def ada(st):
                pe.wait_ge(sg["c_lo"], st.before("c_lo") + 1)
                for m in range(ADA_UNITS):
                    slot, use = st.unit(m)
                    unit_ready(slot, use)
                    if m >= 2:
                        pe.wait_ge(sg["mod_ready"], st.before("mod_ready") + m - 1)
                    else:
                        pe.wait_ge(sg["x_ready"], st.before("x_ready") + TT)
                    row_unit(slot, 4 + m % 2, FU, c_hi, c_lo, range(KT), tiles=1)

            def mix2(st):
                turn_rows(st, y, "h_ready", st.before("h_ready") - TT)
                for job in MIX2_WALK:
                    if job[0] == "unit":
                        m = job[1]
                        unit = MIX2_UNITS[m]
                        slot, use = st.unit(m)
                        unit_ready(slot, use)
                        if m >= 2:
                            pe.wait_ge(sg["proj_copied"], st.before("proj_copied") + m - 1)
                        if unit[0] == "T":
                            turned_unit(slot, 4 + m % 2, sum(w for _, w in unit[1]))
                        elif unit[0] == "N":
                            row_unit(slot, 4 + m % 2, sum(w for _, w in unit[1]), col_hi, col_lo, range(KT))
                        else:
                            if unit == ("UQ", 0):
                                for g in range(2, 4):
                                    b, n = TURNS2["trlat", g][0]
                                    pe.wait_ge(free[b], st.before(free_name[b]) + TT + n + 2)
                            row_unit(slot, 4 + m % 2, 192, lat_hi, lat_lo,
                                     range(6) if unit[0] == "UQ" else range(6, 8))
                    elif job[0] == "idx":
                        i, pairs = IDX_STEPS[job[1]]
                        if job[1] == 0:
                            pe.wait_ge(sg["proj_copied"], st.before("proj_copied") + 3)
                        scores_free(st, job[1])
                        keys = (i + 1) * P
                        for half in range(2):
                            rows = slice(64 * half, 64 * half + 64)
                            for n, j in enumerate(pairs):
                                last = pe.matmul(ps[:, half, n * keys:(n + 1) * keys],
                                                 cols2[rows, C_QI + j, i * P:(i + 1) * P],
                                                 cols2[rows, C_KI, 0:keys], start=True, stop=True)
                            last.then_inc(sg["scores"], 1)
                    elif job[0] == "trlat":
                        i, hf = job[1] // 2, job[1] % 2
                        pe.wait_ge(sg["latent"], st.before("latent") + i + 1)
                        turn_banks(st, TURNS2, job, [(rows2[:, i, (4 * hf + k) * P:(4 * hf + k + 1) * P], k * P)
                                                     for k in range(4)])
                    elif job[0] == "trA":
                        g = job[1]
                        if g == 0:
                            pe.wait_ge(sg["rope_done"], st.before("rope_done") + 1)
                        tiles = []
                        for n in range(2):
                            for i in range(TT):
                                h = 2 * (g % 3) + n
                                src = (rows2[:, i, R_QA + h * A_HD:R_QA + (h + 1) * A_HD] if g < 3
                                       else ka[:, i, h, :])
                                tiles.append((src, (n * TT + i) * P))
                        turn_banks(st, TURNS2, job, tiles)
                    elif job[0] == "score":
                        group, s = job[1:]
                        if s == 0:
                            if group == "A":
                                for g in range(4, 6):
                                    b, n = TURNS2["trA", g][0]
                                    pe.wait_ge(free[b], st.before(free_name[b]) + TT + n + 2)
                                pe.wait_ge(sg["proj_copied"], st.before("proj_copied") + 19)
                            else:
                                pe.wait_ge(sg["proj_copied"], st.before("proj_copied") + {"B": 12, "C": 22}[group])
                        attend_scores(st, group, s)
                    elif job[0] == "turn":
                        attend_turn(st, TURNS2, *job[1:])
                    elif job[0] == "mix":
                        attend_mix(st, TURNS2, *job[1:])
                    elif job[0] == "ycols":
                        y_turn(st, TURNS2, job, YPARTS2)
                    elif job[0] == "out":
                        out_unit(st, TURNS2, job[1], MIX2_PROJ, YPARTS2, 11)

            for j in range(SLOTS):
                pe.sem_inc(used[j], 1)
            pe.wait_ge(ident_in, 16)
            with pe.Fori(0, DEPTH) as l:
                for pos, name in enumerate(STAGES1):
                    st = Stage(1, l, pos)
                    if name == "ffn":
                        ffn(st)
                    if name == "mix1":
                        mix1(st)
            with pe.Fori(0, DEPTH) as l:
                ada(Stage(2, l, 0))
                mix2(Stage(2, l, 1))

        @block.scalar
        def _(act):
            steps = Steps(act, a_steps, a_marks)

            def split(slot, use, n=UNIT, piece=None):
                act.wait_ge(landed[slot], 16 * (use + 1))
                if piece is not None:
                    act.wait_ge(*piece)
                act.wait_ge(used[slot], use + 1)
                act.activation(w_hi[slot][:, 0:n], raw[slot][:, 0:n], ACT.Copy).then_inc(hi_ready[slot], 1)

            def split_unit(st, m, sizes, piece_of=lambda m: None):
                if m < len(sizes):
                    split(*st.unit(m), sizes[m], piece_of(m))
                elif st.block == 1:
                    split(*st.unit(m))

            def cols_hi(st, i, hf, dst, nth):
                act.wait_ge(turned[hf], st.before(f"turned{hf}") + i + 1)
                act.activation(dst[:, 4 * hf:4 * hf + 4, i * P:(i + 1) * P],
                               bank(6 + hf).rearrange("p (k s) -> p k s", k=4), ACT.Copy)\
                   .then_inc(sg["hi_part"], 1)

            def rows_hi(st):
                for i in range(TT):
                    for hf in range(2):
                        cols_hi(st, i, hf, col_hi, 2 * i + hf)

            def turn_wait(st, turns, job, which=0):
                b, n = turns[job][which]
                act.wait_ge(turned[b], st.before(f"turned{b}") + TT + n + 1)
                return b

            def turn_copy(st, turns, job, dst, src_n, which=0, rows=P):
                b = turn_wait(st, turns, job, which)
                act.activation(dst, ps[0:rows, 6 + b, 0:src_n], ACT.Copy).then_inc(free[b], 1)

            def attend_probs(st, group, s, turns):
                _, i, pairs = steps_of(group)[s]
                o_ = ordinal(group, s)
                act.wait_ge(sg["maxed"], st.before("maxed") + o_ + 1)
                if o_ > 0:
                    before = [("turn", s - 1)] if group == "W" else [("turn", g, n) for (g, n), v in ORDER2.items()
                                                                     if v == o_ - 1]
                    for half in range(2):
                        b, n = turns[before[0]][half]
                        act.wait_ge(turned[b], st.before(f"turned{b}") + TT + n + 1)
                keys = (i + 1) * P
                for half in range(2):
                    for n, j in enumerate(pairs):
                        h = head_of(group, j, half)
                        last = act.activation(prob[:, half, n * keys:(n + 1) * keys],
                                              score[:, half, n * keys:(n + 1) * keys], ACT.Exp,
                                              bias=neg_max[:, i, h:h + 1], accum_out=row_sum[:, i, h:h + 1])
                last.then_inc(sg["probs"], 1)

            def attend_copy(st, turns, group, s):
                job = ("turn", s) if group == "W" else ("turn", group, s)
                _, i, pairs = steps_of(group)[s]
                o_ = ordinal(group, s)
                if o_ > 0:
                    act.wait_ge(sg["mixed"], st.before("mixed") + o_)
                n = len(pairs) * (i + 1) * P
                for half in range(2):
                    turn_copy(st, turns, job, prob_t[:, half, 0:n], n, half)

            def y_hi(st, turns, job, parts):
                _, i, part = job
                tiles = parts[part]
                turn_wait(st, turns, job)
                act.activation(col_hi[:, tiles[0]:tiles[-1] + 1, i * P:(i + 1) * P],
                               bank(6 + i, len(tiles) * P).rearrange("p (k s) -> p k s", s=P), ACT.Copy)\
                   .then_inc(sg["hi_part"], 1)

            def ffn(st, last_stage=False):
                g, u, d = st.first, (st.first + 1) % SLOTS, (st.first + 2) % SLOTS
                rows_hi(st)

                def silu(i):
                    act.wait_ge(used[g], st.uses(g) + i + 2)
                    if not isinstance(i, int) or i > 0:
                        act.wait_ge(sg["h_done"], st.before("h_done") + i)
                    act.activation(silu_a, bank(4), ACT.Silu).then_inc(sg["silu_done"], 1)

                def h_hi(i, s_):
                    act.wait_ge(sg["h_done"], st.before("h_done") + i + 1)
                    if s_ == 0 and (not isinstance(i, int) or i > 0):
                        act.wait_ge(used[d], st.uses(d) + i + 1)
                    act.activation(lat_hi[:, 2 * s_:2 * s_ + 2, :].rearrange("p a b -> p (a b)"), hidden, ACT.Copy)\
                       .then_inc(sg["h_hi"], 1)

                silu(0)
                split(g, st.uses(g) + 1)
                split(u, st.uses(u) + 1)
                h_hi(0, 0)
                with steps.loop(1, ROUNDS - 1, f"ffn{st.position}_a") as i:
                    split(d, st.uses(d) + i - 1)
                    silu(i)
                    split(g, st.uses(g) + i + 1)
                    split(u, st.uses(u) + i + 1)
                    h_hi(i, 0)
                i = ROUNDS - 1
                split(d, st.uses(d) + i - 1)
                silu(i)
                split(g, st.uses(g) + ROUNDS)
                if not last_stage:
                    split(u, st.uses(u) + ROUNDS)
                h_hi(i, 1)
                if not last_stage:
                    split(d, st.uses(d) + ROUNDS - 1)

            def mix1(st):
                sizes = [KT * w for _, w in MIX1_COLS] + [UNIT] * OUT_UNITS
                rows_hi(st)
                for job in MIX1_WALK:
                    if job[0] == "unit":
                        m = job[1]
                        split_unit(st, m + 2, sizes)
                        slot, use = st.unit(m)
                        act.wait_ge(used[slot], use + 2)
                        c, w = MIX1_COLS[m]
                        src = bank(4 + m % 2).rearrange("p (t n) -> p t n", t=TT)[:, :, 0:w]
                        dst = rows1[:, :, c:c + w]
                        if m < 2:
                            src = src.rearrange("p t (j d) -> p t j d", j=4)
                            dst = rows1[:, :, QA:KA].rearrange("p t (j f d) -> p t j f d", j=4, f=2)[:, :, :, m, :]
                        act.activation(dst, src, ACT.Silu if c >= GR else ACT.Copy).then_inc(sg["proj_copied"], 1)
                    elif job[0] == "trqk":
                        for i in range(TT):
                            turn_copy(st, TURNS1, job, q1_t[:, :, i * P:(i + 1) * P], HALF, i)
                        turn_copy(st, TURNS1, job, k1_t, S, 2)
                    elif job[0] == "score":
                        attend_probs(st, "W", job[1], TURNS1)
                    elif job[0] == "turn":
                        attend_copy(st, TURNS1, "W", job[1])
                    elif job[0] == "trret":
                        dst, i = (qr_t, kr_t)[job[1] // 2], job[1] % 2
                        turn_copy(st, TURNS1, job, dst[:, :, i * P:(i + 1) * P], HALF)
                    elif job[0] == "attn_out":
                        act.wait_ge(sg["sink_sum"], st.before("sink_sum") + 1)
                        act.activation(sink_e[:, :, :], sink_e[:, :, :], ACT.Exp).then_inc(sg["sink_exp"], 1)
                    elif job[0] == "ycols":
                        y_hi(st, TURNS1, job, YPARTS1)
                    elif job[0] == "out":
                        split_unit(st, MIX1_PROJ + job[1] + 2, sizes)

            def ada(st):
                split_unit(st, 0, [UNIT] * 2)
                split_unit(st, 1, [UNIT] * 2)
                act.wait_ge(sg["x_ready"], st.before("x_ready") + TT)
                act.activation(c_hi, c_silu.unsqueeze(2).to_broadcast([P, KT, P]), ACT.Copy)\
                   .then_inc(sg["c_hi"], 1)
                sizes = [UNIT] * (ADA_UNITS + 2)
                for m in range(ADA_UNITS):
                    split_unit(st, m + 2, sizes)

            def mix2(st):
                sizes = []
                for unit in MIX2_UNITS:
                    if unit[0] in ("T", "N"):
                        sizes.append(KT * sum(w for _, w in unit[1]))
                    else:
                        sizes.append((6 if unit[0] == "UQ" else 2) * 192)
                sizes += [UNIT] * OUT_UNITS
                pieces = lambda m: {2: (k_piece, 16 * (st.layer + 1)), 3: (w_piece, 32 * (st.layer + 1))}.get(m)
                rows_hi(st)
                for job in MIX2_WALK:
                    if job[0] == "unit":
                        m = job[1]
                        unit = MIX2_UNITS[m]
                        split_unit(st, m + 2, sizes, pieces)
                        slot, use = st.unit(m)
                        act.wait_ge(used[slot], use + 2)
                        src = bank(4 + m % 2).rearrange("p (t n) -> p t n", t=TT)
                        if unit[0] == "T":
                            n = sum(w for _, w in unit[1]) // P
                            dst, src = cols2[:, unit[2]:unit[2] + n, :], src[:, 0:n, :]
                        elif unit[0] == "N":
                            w = sum(w for _, w in unit[1])
                            dst, src = rows2[:, :, unit[2]:unit[2] + w], src[:, :, 0:w]
                        elif unit[0] == "UK":
                            dst = ka[:, :, 3 * unit[1]:3 * unit[1] + 3, 0:HD]
                            src = src[:, :, 0:192].rearrange("p t (h d) -> p t h d", h=3)
                        else:
                            c = (R_QA if unit[0] == "UQ" else R_VA) + 192 * unit[1]
                            dst, src = rows2[:, :, c:c + 192], src[:, :, 0:192]
                        act.activation(dst, src, ACT.Copy).then_inc(sg["proj_copied"], 1)
                    elif job[0] == "idx":
                        i, pairs = IDX_STEPS[job[1]]
                        if job[1] > 0:
                            act.wait_ge(sg["idx_summed"], st.before("idx_summed") + job[1])
                        n = len(pairs) * (i + 1) * P
                        for half in range(2):
                            act.wait_ge(sg["scores"], st.before("scores") + 2 * job[1] + half + 1)
                            act.activation(prob[:, half, 0:n], bank(half, n), ACT.Relu).then_inc(sg["score_free"], 1)
                    elif job[0] == "latent":
                        act.wait_ge(sg["proj_copied"], st.before("proj_copied") + 8)
                        junk = prob_t[:, :, :].rearrange("p a b -> p (a b)")
                        for i in range(TT):
                            steps.wait(act.activation(junk[:, 0:Q_LORA], rows2[:, i, R_CQ:R_CKV], ACT.Square,
                                                      accum_out=lat_var[:, 0, i:i + 1]))
                            last = act.activation(junk[:, 0:KV_LORA], rows2[:, i, R_CKV:R_CKV + KV_LORA], ACT.Square,
                                                  accum_out=lat_var[:, 1, i:i + 1])
                            if i < TT - 1:
                                steps.wait(last)
                        last.then_inc(sg["squares"], 1)
                    elif job[0] == "trlat":
                        i, hf = job[1] // 2, job[1] % 2
                        b = turn_wait(st, TURNS2, job)
                        act.activation(lat_hi[:, 4 * hf:4 * hf + 4, i * P:(i + 1) * P],
                                       bank(6 + b).rearrange("p (k s) -> p k s", k=4), ACT.Copy)\
                           .then_inc(sg["hi_part"], 1)
                    elif job[0] == "trA":
                        g = job[1]
                        dst = (qa_t if g < 3 else ka_t)[0:A_HD, 2 * (g % 3):2 * (g % 3) + 2, :]
                        turn_copy(st, TURNS2, job, dst.rearrange("p a b -> p (a b)"), HALF, rows=A_HD)
                    elif job[0] == "score":
                        attend_probs(st, *job[1:], TURNS2)
                    elif job[0] == "turn":
                        attend_copy(st, TURNS2, *job[1:])
                    elif job[0] == "gates":
                        act.wait_ge(sg["proj_copied"], st.before("proj_copied") + MIX2_PROJ)
                        act.activation(rows2[:, :, R_GATE:R_GATE + D], rows2[:, :, R_GATE:R_GATE + D], ACT.Silu)\
                           .then_inc(sg["gates"], 1)
                    elif job[0] == "ycols":
                        y_hi(st, TURNS2, job, YPARTS2)
                    elif job[0] == "out" and job[1] < OUT_UNITS - 2:
                        split_unit(st, MIX2_PROJ + job[1] + 2, sizes)

            for j in range(SLOTS):
                act.sem_inc(hi_ready[j], 1)
            act.wait_ge(c_in, 16)
            act.activation(c_silu, c_raw, ACT.Silu).then_inc(c_ready, 1)
            with steps.loop(0, DEPTH, "layer1_a") as l:
                for pos, name in enumerate(STAGES1):
                    st = Stage(1, l, pos)
                    if pos == 0:
                        split(*st.unit(0))
                        split(*st.unit(1))
                    if name == "ffn":
                        ffn(st, last_stage=pos > 0)
                    if name == "mix1":
                        mix1(st)
            act.wait_ge(c_ready, 1)
            with steps.loop(0, DEPTH, "layer2_a") as l:
                ada(Stage(2, l, 0))
                mix2(Stage(2, l, 1))

        @block.vector
        def _(dve):
            steps = Steps(dve, v_steps, v_marks)
            tt, stt, ts = dve.tensor_tensor, dve.scalar_tensor_tensor, dve.tensor_scalar

            def split(slot, use, n=UNIT):
                dve.wait_ge(hi_ready[slot], use + 2)
                tt(w_lo[slot][:, 0:n], raw[slot][:, 0:n], w_hi[slot][:, 0:n].bitcast(F32), ALU.subtract)\
                    .then_inc(lo_ready[slot], 1)

            def split_unit(st, m, sizes):
                if m < len(sizes):
                    split(*st.unit(m), sizes[m])
                elif st.block == 1:
                    split(*st.unit(m))

            def lo_part(st, nth, src, hi, lo, b):
                dve.wait_ge(sg["hi_part"], st.before("hi_part") + nth + 1)
                tt(lo, src, hi.bitcast(F32), ALU.subtract).then_inc(free[b], 1)

            def rows_lo(st):
                for i in range(TT):
                    for hf in range(2):
                        tiles, toks = slice(4 * hf, 4 * hf + 4), slice(i * P, (i + 1) * P)
                        lo_part(st, 2 * i + hf, bank(6 + hf).rearrange("p (k s) -> p k s", k=4),
                                col_hi[:, tiles, toks], col_lo[:, tiles, toks], hf)

            def y_lo(st, job, parts, nth):
                _, i, part = job
                tiles, toks = slice(parts[part][0], parts[part][-1] + 1), slice(i * P, (i + 1) * P)
                lo_part(st, nth, bank(6 + i, len(parts[part]) * P).rearrange("p (k s) -> p k s", s=P),
                        col_hi[:, tiles, toks], col_lo[:, tiles, toks], i)

            def norm(st, banks, params):
                for i in range(TT):
                    dve.wait_ge(sg["sum_ready"], st.before("sum_ready") - TT + i + 1)
                    total = ps[:, banks[i]:banks[i] + 2, :]
                    xi = x[:, i, :].rearrange("p (a b) -> p a b", a=2)
                    yi = y[:, i, :].rearrange("p (a b) -> p a b", a=2)
                    if st.block == 2:
                        gate = mod[:, 2 * D:3 * D].rearrange("p (a b) -> p a b", a=2)
                        steps.wait(tt(yi, total, gate, ALU.mult))
                        total = yi
                    steps.wait(stt(yi, xi, ALPHA, total, ALU.mult, ALU.add))
                    dve.bn_stats(stats[:, i, 0, :], y[:, i, 0:HALF])
                    steps.wait(dve.bn_stats(stats[:, i, 1, :], y[:, i, HALF:D]))
                    steps.settle()
                    steps.wait(dve.bn_aggr(mean_var[:, i, :], stats[:, i, :, :]))
                    ts(mean_var[:, i, 1:2], mean_var[:, i, 1:2], LN_EPS, None, ALU.add).then_inc(sg["var_ready"], 1)
                    if i == 0:
                        dve.wait_ge(params_in, params)
                    steps.wait(stt(y[:, i, :], y[:, i, :], mean_var[:, i, 0:1], norm_g[:, :], ALU.subtract, ALU.mult))
                    dve.wait_ge(sg["rstd_ready"], st.before("rstd_ready") + i + 1)
                    stt(x[:, i, :], y[:, i, :], rstd[:, i:i + 1], norm_b[:, :], ALU.mult, ALU.add)\
                        .then_inc(sg["x_ready"], 1)

            def ffn(st, last_stage=False):
                g, u, d = st.first, (st.first + 1) % SLOTS, (st.first + 2) % SLOTS
                rows_lo(st)

                def h(i):
                    dve.wait_ge(sg["silu_done"], st.before("silu_done") + i + 1)
                    dve.wait_ge(used[u], st.uses(u) + i + 2)
                    if not isinstance(i, int) or i > 0:
                        dve.wait_ge(sg["h_lo"], st.before("h_lo") + i)
                    stt(hidden, silu_a, 0.5, bank(5), ALU.mult, ALU.mult).then_inc(sg["h_done"], 1)

                def h_lo(i, s_):
                    dve.wait_ge(sg["h_hi"], st.before("h_hi") + i + 1)
                    tiles = slice(2 * s_, 2 * s_ + 2)
                    tt(lat_lo[:, tiles, :].rearrange("p a b -> p (a b)"), hidden,
                       lat_hi[:, tiles, :].rearrange("p a b -> p (a b)").bitcast(F32), ALU.subtract)\
                        .then_inc(sg["h_lo"], 1)

                split(g, st.uses(g) + 1)
                h(0)
                split(u, st.uses(u) + 1)
                h_lo(0, 0)
                with steps.loop(1, ROUNDS - 1, f"ffn{st.position}_v") as i:
                    split(d, st.uses(d) + i - 1)
                    split(g, st.uses(g) + i + 1)
                    h(i)
                    split(u, st.uses(u) + i + 1)
                    h_lo(i, 0)
                i = ROUNDS - 1
                split(d, st.uses(d) + i - 1)
                split(g, st.uses(g) + ROUNDS)
                h(i)
                if not last_stage:
                    split(u, st.uses(u) + ROUNDS)
                h_lo(i, 1)
                if not last_stage:
                    split(d, st.uses(d) + ROUNDS - 1)

            def rope(x1, x2, whole, cos, sin, shape, cos_whole, tmp1, tmp2):
                tt(tmp1, x2, sin.to_broadcast(shape), ALU.mult)
                steps.wait(tt(tmp2, x1, sin.to_broadcast(shape), ALU.mult))
                steps.wait(tt(whole, whole, cos_whole, ALU.mult))
                tt(x1, x1, tmp1, ALU.subtract)
                return tt(x2, x2, tmp2, ALU.add)

            def attend_max(st, group, s):
                _, i, pairs = steps_of(group)[s]
                o_, before, keys, n = ordinal(group, s), scored_before(group, s), (i + 1) * P, len(pairs)
                if o_ > 0:
                    dve.wait_ge(sg["probs"], st.before("probs") + o_)
                scale = A_HD ** -0.5 if group == "A" else HD ** -0.5
                window = slice(2 * P - keys, 2 * P)
                for half in range(2):
                    dve.wait_ge(sg["scores"], st.before("scores") + 2 * before + half + 1)
                    if group in "WA":
                        bias = table[:, 0:256][:, window].unsqueeze(1).to_broadcast([P, n, keys])
                    else:
                        at_, per = (T2_B, 3) if group == "B" else (T2_C, 2)
                        bias = table[:, at_ + half * per * 256:at_ + (half + 1) * per * 256]\
                            .rearrange("p (j s) -> p j s", j=per)[:, pairs[0]:pairs[-1] + 1, window]
                    dst = score[:, half, 0:n * keys].rearrange("p (j s) -> p j s", j=n)
                    last = stt(dst, bank(half, n * keys).rearrange("p (j s) -> p j s", j=n), scale, bias,
                               ALU.mult, ALU.add)
                    last.then_inc(sg["score_free"], 1)
                    dve.wait_ge(sg["score_free"], st.before("score_free") + 2 * before + half + 1)
                    if group == "C":
                        steps.wait(tt(dst, dst, not_taken[:, i, 0:keys].unsqueeze(1).to_broadcast([P, n, keys]),
                                      ALU.add))
                steps.wait(dve.tensor_reduce(by_pair(row_max, i, group, pairs),
                                             score[:, :, 0:n * keys].rearrange("p f (j s) -> p f j s", j=n),
                                             AX_X, ALU.max))
                top = by_pair(row_max, i, group, pairs)
                if group == "W":
                    steps.wait(tt(top, top, sinks.rearrange("p (f j) -> p f j", f=2)[:, :, pairs[0]:pairs[-1] + 1],
                                  ALU.max))
                ts(by_pair(neg_max, i, group, pairs), top, -1.0, None, ALU.mult).then_inc(sg["maxed"], 1)

            def read_out(st, group, i, col, signal):
                heads = group_heads(group)
                steps.wait(dve.reciprocal(row_inv[:, i, 0:heads], row_sum[:, i, 0:heads]))
                return tt(y[:, i, col:col + heads * HD].rearrange("p (h d) -> p h d", h=heads),
                          bank(2 + i, heads * HD).rearrange("p (h d) -> p h d", h=heads),
                          row_inv[:, i, 0:heads].unsqueeze(2).to_broadcast([P, heads, HD]), ALU.mult)

            def mix1(st):
                sizes = [KT * w for _, w in MIX1_COLS] + [UNIT] * OUT_UNITS
                rows_lo(st)
                for job in MIX1_WALK:
                    if job[0] == "unit":
                        split_unit(st, job[1] + 2, sizes)
                    elif job[0] == "rope1":
                        dve.wait_ge(sg["proj_copied"], st.before("proj_copied") + 3)
                        heads = ATTN1_HEADS + KV1_HEADS
                        for i in range(TT):
                            v = rows1[:, i, QA:VA].rearrange("p (h f d) -> p h f d", h=heads, f=2)
                            cos, sin = (table[:, T1_ROPE + 64 * i + c:T1_ROPE + 64 * i + c + 32] for c in (0, 32))
                            tmp = score[:, :, 0:320].rearrange("p f (h d) -> p f h d", h=heads)
                            tmp = [tmp[:, f, :, :] for f in range(2)]
                            last = rope(v[:, :, 0, :], v[:, :, 1, :], v, None, sin.unsqueeze(1), [P, heads, 32],
                                        cos.unsqueeze(1).unsqueeze(1).to_broadcast([P, heads, 2, 32]), *tmp)
                            if i < TT - 1:
                                steps.wait(last)
                        last.then_inc(sg["rope_done"], 1)
                    elif job[0] == "score":
                        if job[1] == 0:
                            dve.wait_ge(sinks_in, 16 * (st.layer + 1))
                        attend_max(st, "W", job[1])
                    elif job[0] == "attn_out":
                        dve.wait_ge(sg["probs"], st.before("probs") + 3)
                        tt(sink_e[:, :, :], neg_max[:, :, :], sinks.unsqueeze(1).to_broadcast([P, TT, 8]), ALU.add)\
                            .then_inc(sg["sink_sum"], 1)
                        dve.wait_ge(sg["sink_exp"], st.before("sink_exp") + 1)
                        steps.wait(tt(row_sum[:, :, :], row_sum[:, :, :], sink_e[:, :, :], ALU.add))
                        dve.wait_ge(sg["mixed"], st.before("mixed") + 3)
                        for i in range(TT):
                            read_out(st, "W", i, 0, None).then_inc(sg["out_copied"], 1)
                        dve.wait_ge(sg["out_copied"], st.before("out_copied") + TT)
                        dve.sem_inc(sg["y_ready"], TT)
                    elif job[0] == "ret":
                        j = job[1]
                        decayed = prob if j % 2 == 0 else score
                        if j >= 2:
                            dve.wait_ge(sg["ret_mixed"], st.before("ret_mixed") + j - 1)
                        decay = table[:, T1_DECAY:T1_ROPE].rearrange("p (f j s) -> p f j s", f=2, j=4)
                        dve.wait_ge(sg["scores"], st.before("scores") + 2 * (3 + j) + 2)
                        tt(decayed[:, :, 0:S], ps[:, 0:2, 0:S], decay[:, :, j, :], ALU.mult)
                        tt(decayed[:, :, S:S + P], ps[:, 0:2, S:S + P], decay[:, :, j, 0:P], ALU.mult)\
                            .then_inc(sg["score_free"], 2)
                    elif job[0] == "groupnorm":
                        dve.wait_ge(sg["ret_mixed"], st.before("ret_mixed") + 4)
                        dve.wait_ge(sg["proj_copied"], st.before("proj_copied") + MIX1_PROJ)
                        heads = lambda v: v.rearrange("p (h d) -> p h d", h=8)
                        wide = lambda v: v.unsqueeze(2).to_broadcast([P, 8, HD])
                        square = heads(score[:, 0, :])
                        for i in range(TT):
                            o_, yr = heads(bank(2 + i)), heads(y[:, i, HALF:D])
                            steps.wait(dve.tensor_reduce(gn_sum[:, i, :], o_, AX_X, ALU.add))
                            steps.wait(ts(gn_sum[:, i, :], gn_sum[:, i, :], 1.0 / HD, None, ALU.mult))
                            steps.wait(tt(yr, o_, wide(gn_sum[:, i, :]), ALU.subtract))
                            steps.wait(tt(square, yr, yr, ALU.mult))
                            steps.wait(dve.tensor_reduce(gn_var[:, i, :], square, AX_X, ALU.add))
                            ts(gn_var[:, i, :], gn_var[:, i, :], 1.0 / HD, GN_EPS, ALU.mult, ALU.add)\
                                .then_inc(sg["var_ready"], 1)
                            steps.wait(tt(yr, yr, heads(rows1[:, i, GR:IN1]), ALU.mult))
                        for i in range(TT):
                            yr = heads(y[:, i, HALF:D])
                            dve.wait_ge(sg["rstd_ready"], st.before("rstd_ready") + i + 1)
                            tt(yr, yr, wide(gn_rstd[:, i, :]), ALU.mult).then_inc(sg["y_ready"], 1)
                    elif job[0] == "ycols":
                        y_lo(st, job, YPARTS1, 2 * TT + 2 * job[2] + job[1])
                    elif job[0] == "out":
                        split_unit(st, MIX1_PROJ + job[1] + 2, sizes)

            def ada(st):
                split_unit(st, 0, [UNIT] * 2)
                split_unit(st, 1, [UNIT] * 2)
                dve.wait_ge(sg["c_hi"], st.before("c_hi") + 1)
                tt(c_lo, c_silu.unsqueeze(2).to_broadcast([P, KT, P]), c_hi.bitcast(F32), ALU.subtract)\
                    .then_inc(sg["c_lo"], 1)
                dve.wait_ge(mod_in, 16 * (st.layer + 1))
                for m in range(ADA_UNITS):
                    split_unit(st, m + 2, [UNIT] * (ADA_UNITS + 2))
                    slot, use = st.unit(m)
                    dve.wait_ge(used[slot], use + 2)
                    cols = slice(m * FU, (m + 1) * FU)
                    one = 0.0 if m < ADA_UNITS // 3 else 1.0
                    stt(mod[:, cols], bank(4 + m % 2, FU), one, mod[:, cols], ALU.add, ALU.add)\
                        .then_inc(sg["mod_ready"], 1)
                dve.wait_ge(sg["mod_ready"], st.before("mod_ready") + ADA_UNITS)
                for i in range(TT):
                    steps.wait(tt(y[:, i, :], x[:, i, :], mod[:, D:2 * D], ALU.mult))
                    tt(y[:, i, :], y[:, i, :], mod[:, 0:D], ALU.add).then_inc(sg["h_ready"], 1)

            def mix2(st):
                sizes = []
                for unit in MIX2_UNITS:
                    if unit[0] in ("T", "N"):
                        sizes.append(KT * sum(w for _, w in unit[1]))
                    else:
                        sizes.append((6 if unit[0] == "UQ" else 2) * 192)
                sizes += [UNIT] * OUT_UNITS
                done = {}
                rows_lo(st)
                y_jobs = [j for j in MIX2_WALK if j[0] == "ycols"]
                for job in MIX2_WALK:
                    if job[0] == "unit":
                        split_unit(st, job[1] + 2, sizes)
                    elif job[0] == "idxw":
                        dve.wait_ge(sg["proj_copied"], st.before("proj_copied") + 4)
                        steps.wait(ts(idx_w[:, :, :], rows2[:, :, R_WI:R_WI + 8], IDX_HEADS ** -0.5 * 64 ** -0.5,
                                      None, ALU.mult))
                        dve.wait_ge(tables_in, 32)
                        for i in range(TT):
                            keys = (i + 1) * P
                            last = dve.tensor_copy(idx_score[:, i, 0:keys], table[:, 2 * P - keys:2 * P])
                        steps.wait(last)
                    elif job[0] == "idx":
                        i, pairs = IDX_STEPS[job[1]]
                        keys = (i + 1) * P
                        for half in range(2):
                            dve.wait_ge(sg["score_free"], st.before("score_free") + 2 * job[1] + half + 1)
                            for n, j in enumerate(pairs):
                                h = 2 * j + half
                                last = stt(idx_score[:, i, 0:keys], prob[:, half, n * keys:(n + 1) * keys],
                                           idx_w[:, i, h:h + 1], idx_score[:, i, 0:keys], ALU.mult, ALU.add)
                                if (half, j) != (1, pairs[-1]):
                                    steps.wait(last)
                        last.then_inc(sg["idx_summed"], 1)
                    elif job[0] == "topk":
                        i = job[1]
                        keys = (i + 1) * P
                        if i == 0:
                            dve.wait_ge(sg["idx_summed"], st.before("idx_summed") + 3)
                        cur = idx_score[:, i, 0:keys]
                        for _ in range(TOPK // 8):
                            steps.settle()
                            steps.wait(dve.max(top8, cur))
                            steps.settle()
                            steps.wait(dve.match_replace(cur, top8, cur, TAKEN))
                        steps.wait(ts(not_taken[:, i, 0:keys], cur, TAKEN / 2, NEG, ALU.is_gt, ALU.mult))
                    elif job[0] == "latent":
                        dve.wait_ge(sg["squares"], st.before("squares") + 1)
                        ts(lat_var[:, 0, :], lat_var[:, 0, :], 1.0 / Q_LORA, RMS_EPS, ALU.mult, ALU.add)
                        ts(lat_var[:, 1, :], lat_var[:, 1, :], 1.0 / KV_LORA, RMS_EPS, ALU.mult, ALU.add)\
                            .then_inc(sg["var_ready"], 1)
                        dve.wait_ge(sg["rstd_ready"], st.before("rstd_ready") + 1)
                        dve.wait_ge(lat_g_in, 32 * (st.layer + 1))
                        for i in range(TT):
                            for a, (c, n) in enumerate(((R_CQ, Q_LORA), (R_CKV, KV_LORA))):
                                last = stt(rows2[:, i, c:c + n], rows2[:, i, c:c + n], lat_rstd[:, a, i:i + 1],
                                           norm_b[:, c:c + n], ALU.mult, ALU.mult)
                                if a == 0:
                                    steps.wait(last)
                            last.then_inc(sg["latent"], 1)
                    elif job[0] == "trlat":
                        i, hf = job[1] // 2, job[1] % 2
                        tiles, toks = slice(4 * hf, 4 * hf + 4), slice(i * P, (i + 1) * P)
                        b = TURNS2[job][0][0]
                        lo_part(st, 2 * TT + job[1], bank(6 + b).rearrange("p (k s) -> p k s", k=4),
                                lat_hi[:, tiles, toks], lat_lo[:, tiles, toks], b)
                    elif job[0] == "ropeA":
                        dve.wait_ge(sg["proj_copied"], st.before("proj_copied") + 17)
                        for i in range(TT):
                            cos, sin = (table[:, T2_ROPE + 32 * i + c:T2_ROPE + 32 * i + c + 16] for c in (0, 16))
                            q = rows2[:, i, R_QA:R_QA + A_HEADS * A_HD].rearrange("p (h d) -> p h d", h=A_HEADS)
                            q = q[:, :, A_NOPE:A_HD].rearrange("p h (f d) -> p h f d", f=2)
                            tmp = rope_tmp[:, 0:192].rearrange("p (f h d) -> p f h d", f=2, h=A_HEADS)
                            steps.wait(rope(q[:, :, 0, :], q[:, :, 1, :], q, None, sin.unsqueeze(1), [P, A_HEADS, 16],
                                            cos.unsqueeze(1).unsqueeze(1).to_broadcast([P, A_HEADS, 2, 16]),
                                            tmp[:, 0, :, :], tmp[:, 1, :, :]))
                            k = rows2[:, i, R_KR:R_KR + A_ROPE].rearrange("p (f d) -> p f d", f=2)
                            steps.wait(rope(k[:, 0, :], k[:, 1, :], k, None, sin, [P, 16],
                                            cos.unsqueeze(1).to_broadcast([P, 2, 16]),
                                            rope_tmp[:, 0:16], rope_tmp[:, 16:32]))
                            last = dve.tensor_copy(ka[:, i, :, A_NOPE:A_HD],
                                                   rows2[:, i, R_KR:R_KR + A_ROPE].unsqueeze(1)
                                                   .to_broadcast([P, A_HEADS, A_ROPE]))
                        last.then_inc(sg["rope_done"], 1)
                    elif job[0] == "score":
                        attend_max(st, *job[1:])
                    elif job[0] == "mix":
                        group, s = job[1:]
                        if s in (0, len(STEPS2[group]) - 1):
                            i = 0 if s == 0 else 1
                            dve.wait_ge(sg["mixed"], st.before("mixed") + ORDER2[group, s] + 1)
                            col = {"A": 0, "B": 384, "C": 768}[group]
                            read_out(st, group, i, col, None).then_inc(sg["out_copied"], 1)
                    elif job[0] == "ycols":
                        _, i, part = job
                        if y_jobs.index(job) == 0:
                            dve.wait_ge(sg["gates"], st.before("gates") + 1)
                            dve.wait_ge(sg["out_copied"], st.before("out_copied") + 6)
                        cols = slice(YPARTS2[part][0] * P, (YPARTS2[part][-1] + 1) * P)
                        tt(y[:, i, cols], y[:, i, cols], rows2[:, i, R_GATE:R_GATE + D][:, cols], ALU.mult)\
                            .then_inc(sg["y_ready"], 1)
                        y_lo(st, job, YPARTS2, 2 * TT + 4 + y_jobs.index(job))
                    elif job[0] == "out" and job[1] < OUT_UNITS - 2:
                        split_unit(st, MIX2_PROJ + job[1] + 2, sizes)

            for j in range(SLOTS):
                dve.sem_inc(lo_ready[j], 1)
            for b in range(2):
                dve.sem_inc(free[b], 1)
            dve.memset(minus_half, -0.5).then_inc(const_ready, 1)
            dve.wait_ge(x_landed, 16)
            dve.sem_inc(sg["x_ready"], TT)
            dve.wait_ge(tables_in, 16)
            with steps.loop(0, DEPTH, "layer1_v") as l:
                for pos, name in enumerate(STAGES1):
                    st = Stage(1, l, pos)
                    if pos == 0:
                        split(*st.unit(0))
                        split(*st.unit(1))
                    if name == "ffn":
                        ffn(st, last_stage=pos > 0)
                    elif name == "mix1":
                        mix1(st)
                    else:
                        norm(st, (0, 4) if STAGES1[pos - 1] == "mix1" else (0, 2), 32 * (3 * l + pos // 2 + 1))
            with steps.loop(0, DEPTH, "layer2_v") as l:
                ada(Stage(2, l, 0))
                mix2(Stage(2, l, 1))
                norm(Stage(2, l, 2), (0, 4), 32 * (3 * DEPTH + l + 1))

        @block.gpsimd
        def _(pool):
            steps = Steps(pool, g_steps, p_marks)

            def params(l, g, b):
                steps.settle()
                pool.dma_start(norm_g[:, :], g[l].partition_broadcast(P)).then_inc(params_in, 16)
                pool.dma_start(norm_b[:, :], b[l].partition_broadcast(P)).then_inc(params_in, 16)

            def norm(st):
                for i in range(TT):
                    pool.wait_ge(sg["var_ready"], st.before("var_ready") + i + 1)
                    pool.tensor_tensor(rstd[:, i:i + 1], mean_var[:, i, 1:2], minus_half[:, 0:1], ALU.pow)\
                        .then_inc(sg["rstd_ready"], 1)

            def rotate(st):
                pool.wait_ge(sg["proj_copied"], st.before("proj_copied") + 7)
                heads = 2 * RET_HEADS
                for i in range(TT):
                    v = rows1[:, i, QR:VR].rearrange("p (h d f) -> p h d f", h=heads, f=2)
                    cos, sin = (table[:, T1_RET + 64 * i + c:T1_RET + 64 * i + c + 32] for c in (0, 32))
                    tmp = rot_tmp.rearrange("p (f h d) -> p f h d", f=2, h=heads)
                    wide = lambda a: a.unsqueeze(1).to_broadcast([P, heads, 32])
                    pool.tensor_tensor(tmp[:, 0, :, :], v[:, :, :, 1], wide(sin), ALU.mult)
                    steps.wait(pool.tensor_tensor(tmp[:, 1, :, :], v[:, :, :, 0], wide(sin), ALU.mult))
                    pool.tensor_tensor(v[:, :, :, 0], v[:, :, :, 0], wide(cos), ALU.mult)
                    steps.wait(pool.tensor_tensor(v[:, :, :, 1], v[:, :, :, 1], wide(cos), ALU.mult))
                    pool.tensor_tensor(v[:, :, :, 0], v[:, :, :, 0], tmp[:, 0, :, :], ALU.subtract)
                    last = pool.tensor_tensor(v[:, :, :, 1], v[:, :, :, 1], tmp[:, 1, :, :], ALU.add)
                    if i < TT - 1:
                        steps.wait(last)
                last.then_inc(sg["rotated"], 1)

            pool.dma_start(x[:, :, :], t["x"][0].rearrange("(t p) d -> p t d", p=P)).then_inc(x_landed, 16)
            pool.dma_start(ident[:, :], t["ident"]).then_inc(ident_in, 16)
            pool.dma_start(table[:, 0:T1], t["table1"]).then_inc(tables_in, 16)
            pool.dma_start(c_raw, t["c_2"][0].rearrange("(k p) -> p k", p=P),
                           allow_slow_non_contiguous=True).then_inc(c_in, 16)
            pool.wait_ge(const_ready, 1)
            with steps.loop(0, DEPTH, "layer1_g") as l:
                for pos, name in enumerate(STAGES1):
                    st = Stage(1, l, pos)
                    if name in ("ffn", "mix1"):
                        pool.wait_ge(sg["x_ready"], st.before("x_ready") + TT)
                        n = pos // 2 + 1
                        params(l, t[f"ln{n}_g"], t[f"ln{n}_b"])
                    if name == "mix1":
                        pool.dma_start(sinks, t["attn_sinks"][l].partition_broadcast(P)).then_inc(sinks_in, 16)
                        rotate(st)
                        for i in range(TT):
                            pool.wait_ge(sg["var_ready"], st.before("var_ready") + i + 1)
                            pool.tensor_tensor(gn_rstd[:, i, :], gn_var[:, i, :], minus_half, ALU.pow)\
                                .then_inc(sg["rstd_ready"], 1)
                    if name == "norm":
                        norm(st)
            pool.wait_ge(sg["x_ready"], TT + signals_before(2, 0, 0, "x_ready"))
            pool.dma_start(table[:, 0:T2], t["table2"]).then_inc(tables_in, 16)
            with steps.loop(0, DEPTH, "layer2_g") as l:
                st = Stage(2, l, 0)
                pool.wait_ge(sg["x_ready"], st.before("x_ready") + TT)
                steps.settle()
                pool.dma_start(mod[:, :], t["b_ada_2"][l].partition_broadcast(P)).then_inc(mod_in, 16)
                pool.dma_start(norm_b[:, 0:Q_LORA], t["q_norm_g_2"][l].partition_broadcast(P)).then_inc(lat_g_in, 16)
                pool.dma_start(norm_b[:, Q_LORA:D], t["kv_norm_g_2"][l].partition_broadcast(P)).then_inc(lat_g_in, 16)
                st = Stage(2, l, 1)
                pool.wait_ge(sg["var_ready"], st.before("var_ready") + 1)
                pool.tensor_tensor(lat_rstd, lat_var, minus_half[:, 0:4].rearrange("p (a t) -> p a t", a=2), ALU.pow)\
                    .then_inc(sg["rstd_ready"], 1)
                pool.wait_ge(sg["latent"], st.before("latent") + TT)
                params(l, t["ln_g_2"], t["ln_b_2"])
                norm(Stage(2, l, 2))


def kernel(**inputs):
    import concourse.bacc as bacc
    from concourse.bass_utils import run_bass_kernel_spmd

    nc = bacc.Bacc("TRN2", target_bir_lowering=False, num_devices=1)
    arrays = {f"in_{k}": np.ascontiguousarray(v) for k, v in inputs.items()}
    for name, table in zip(("table1", "table2", "ident"), shape_tables()):
        arrays[f"in_{name}"] = table
    t = {k[3:]: nc.dram_tensor(k, v.shape, mybir.dt.from_np(v.dtype), kind="ExternalInput").ap()
         for k, v in arrays.items()}
    out = nc.dram_tensor("out_0", (1, S, D), F32, kind="ExternalOutput").ap()
    build(nc, t, out)
    result = run_bass_kernel_spmd(nc, [arrays], core_ids=[0])
    return result.results[0]["out_0"]
```

```python
import math
from contextlib import ExitStack

import numpy as np

import concourse.bass as bass
from concourse import mybir

F32 = mybir.dt.float32
F32R = mybir.dt.float32r
ALU = mybir.AluOpType
ACT = mybir.ActivationFunctionType
AX_X = mybir.AxisListType.X

P = 128
S = 256
TT = S // P
D = 1024
KT = D // P
HD = 64
DEPTH = 2
F = 2816
FU = 256
ROUNDS = F // FU
SLOTS = 3
UNIT = KT * FU
HALF = 512
ALPHA = (2 * DEPTH) ** 0.25
LN_EPS = 1e-5
GN_EPS = 1e-6
RMS_EPS = 1e-6
NEG = -1e30
TAKEN = -3e38
TOPK = min(256, S // 4)

ATTN1_HEADS, KV1_HEADS, RET_HEADS = 8, 2, 8
QA, KA, VA, QR, KR, VR, GR = 0, 512, 640, 768, 1280, 1792, 2304
IN1 = 2816
MIX1_COLS = [(c, 256) for c in range(0, IN1, 256)] + [(IN1 - 256, 256)]
HALF_KT = KT // 2
MIX1_PROJ = len(MIX1_COLS)

A_HEADS, A_NOPE, A_ROPE, B_HEADS, C_HEADS, IDX_HEADS = 6, 64, 32, 6, 4, 8
A_HD = A_NOPE + A_ROPE
CQ, CKV, KROPE, QB, KB, VB, QC, KC, VC, QI, KI, WI, GATE = (
    0, 768, 1024, 1056, 1440, 1824, 2208, 2464, 2720, 2976, 3488, 3552, 3560)
Q_LORA, KV_LORA = 768, 256

R_CQ, R_CKV = 0, 768
R_QA, R_VA = 0, 576
R_VB, R_KR, R_WI = 1024, 1408, 1440
R_VC, R_GATE = 1448, 1704
R_ROW = 2728
C_QI, C_KI, C_QKB, C_QKC = 0, 4, 5, 11
C_TILES = 15

MIX2_UNITS = [
    ("T", [(QI, 256)], C_QI), ("T", [(QI + 256, 256)], C_QI + 2),
    ("T", [(KI, 64), (KI, 64)], C_KI),
    ("N", [(VB + 256, 128), (KROPE, 32), (WI, 8)], R_VB + 256),
    ("T", [(QB, 256)], C_QKB), ("T", [(QB + 256, 256)], C_QKB + 2), ("T", [(QB + 512, 256)], C_QKB + 4),
    ("N", [(VB, 256)], R_VB),
    ("N", [(CQ, 256)], R_CQ), ("N", [(CQ + 256, 256)], R_CQ + 256), ("N", [(CQ + 512, 256)], R_CQ + 512),
    ("N", [(CKV, 256)], R_CKV),
    ("T", [(QC, 256)], C_QKC), ("T", [(QC + 256, 256)], C_QKC + 2),
    ("N", [(VC, 256)], R_VC),
    ("UQ", 0), ("UQ", 1), ("UQ", 2), ("UK", 0), ("UK", 1), ("UV", 0), ("UV", 1),
    ("N", [(GATE, 256)], R_GATE), ("N", [(GATE + 256, 256)], R_GATE + 256),
    ("N", [(GATE + 512, 256)], R_GATE + 512), ("N", [(GATE + 768, 256)], R_GATE + 768),
]
UNITS_IDX_W, UNITS_B, UNITS_LATENT, UNITS_C = 4, 8, 12, 14
UNITS_UQ, UNITS_UK, UNITS_UV = 18, 20, 22
MIX2_PROJ = len(MIX2_UNITS)
OUT_UNITS = 4
MOD = 3 * D
MOD_CHUNKS = 2 * (ROUNDS - 3)
MOD_W = MOD // MOD_CHUNKS

STEPS1 = [("W", 0, (0, 1, 2, 3)), ("W", 1, (0, 1)), ("W", 1, (2, 3))]
STEPS2 = {"B": [("B", 0, (0, 1, 2)), ("B", 1, (0, 1)), ("B", 1, (2,))],
          "A": [("A", 0, (0, 1, 2)), ("A", 1, (0, 1)), ("A", 1, (2,))],
          "C": [("C", 0, (0, 1)), ("C", 1, (0, 1))]}
IDX_STEPS = [(0, (0, 1, 2, 3)), (1, (0, 1)), (1, (2, 3))]

MIX1_WALK = (
    [("unit", 0), ("unit", 1), ("unit", 2), ("rope1",), ("unit", 3), ("trqk",),
     ("unit", 4), ("score", 0), ("unit", 5), ("unit", 6), ("turn", 0), ("score", 1), ("unit", 7), ("mix", 0),
     ("unit", 8), ("turn", 1), ("score", 2), ("trret", 0), ("trret", 1), ("unit", 9), ("mix", 1),
     ("trret", 2), ("trret", 3), ("turn", 2), ("ret", 0), ("unit", 10), ("mix", 2), ("ret", 1), ("attn_out",),
     ("unit", 11), ("retmix", 0), ("ret", 2), ("retmix", 1), ("ret", 3),
     ("ycols", 0, 0), ("ycols", 1, 0), ("retmix", 2), ("retmix", 3),
     ("groupnorm",), ("out", 0), ("out", 1), ("ycols", 0, 1), ("ycols", 1, 1), ("out", 2), ("out", 3)])

MIX2_WALK = (
    [("unit", 0), ("unit", 1), ("unit", 2), ("unit", 3), ("idxw",),
     ("unit", 4), ("idx", 0), ("unit", 5), ("idx", 1), ("unit", 6), ("idx", 2), ("unit", 7), ("topk", 0, 0), ("topk", 0, 1),
     ("unit", 8), ("score", "B", 0), ("topk", 0, 2), ("topk", 0, 3), ("unit", 9), ("ropeK",), ("topk", 1, 0),
     ("unit", 10), ("turn", "B", 0), ("score", "B", 1), ("topk", 1, 1), ("unit", 11), ("mix", "B", 0),
     ("topk", 1, 2), ("topk", 1, 3), ("unit", 12), ("latent",), ("turn", "B", 1), ("score", "B", 2),
     ("unit", 13), ("mix", "B", 1), ("trlat", 0), ("trlat", 1),
     ("unit", 14), ("turn", "B", 2), ("trlat", 2), ("trlat", 3), ("score", "C", 0),
     ("unit", 15), ("mix", "B", 2), ("unit", 16), ("turn", "C", 0), ("score", "C", 1), ("unit", 17), ("mix", "C", 0),
     ("unit", 18), ("ropeA",), ("unit", 19), ("turn", "C", 1), ("trA", 0), ("trA", 1), ("unit", 20), ("trA", 2), ("trA", 3),
     ("mix", "C", 1), ("trA", 4), ("trA", 5), ("score", "A", 0), ("unit", 21), ("unit", 22),
     ("turn", "A", 0), ("score", "A", 1), ("unit", 23), ("mix", "A", 0), ("unit", 24),
     ("turn", "A", 1), ("score", "A", 2), ("unit", 25), ("mix", "A", 1),
     ("turn", "A", 2), ("gates",), ("mix", "A", 2),
     ("ycols", 0, 0), ("ycols", 1, 0), ("ycols", 0, 1), ("ycols", 1, 1),
     ("out", 0), ("out", 1), ("out", 2), ("ycols", 0, 2), ("ycols", 1, 2), ("out", 3)])
TOPK_PARTS = 4
YPARTS1 = [(0, 1, 2, 3), (4, 5, 6, 7)]
YPARTS2 = [(0, 1, 2), (3, 4, 5), (6, 7)]


def ps_turns(walk):
    turns, n = {}, [0, 0]
    for job in walk:
        banks = {"turn": (0, 1), "trqk": (0, 1, 0), "trlat": (0,), "trA": (0,), "trret": (0,),
                 "ycols": (0,)}.get(job[0], ())
        if job[0] in ("trlat", "trA", "trret"):
            banks = (job[1] % 2,)
        if job[0] == "ycols":
            banks = (job[1],)
        got = []
        for b in banks:
            got.append((b, n[b]))
            n[b] += 1
        if got:
            turns[job] = got
    return turns, n


TURNS1, NTURNS1 = ps_turns(MIX1_WALK)
TURNS2, NTURNS2 = ps_turns(MIX2_WALK)

IDLE_IN, IDLE_OPEN = 3200, 7000
IDLE_COND, IDLE_COND_SPLIT = 7500, 3500
IDLE_START = 6000
IDLE_RETMIX, IDLE_GATED = 1000, 2000

STAGES1 = ["ffn", "norm", "mix1", "norm", "ffn", "norm"]
STAGES2 = ["cond", "mix2", "norm"]
SIGNALS = {
    "ffn": dict(turned0=TT, turned1=TT, free0=TT, free1=TT, hi_part=2 * TT, silu_done=ROUNDS, h_done=ROUNDS,
                h_hi=ROUNDS, h_lo=ROUNDS, sum_ready=TT, mod_summed=MOD_CHUNKS // 2,
                mod_spread=MOD_CHUNKS // 2, mod_row=MOD_CHUNKS // 2),
    "norm": dict(var_ready=TT, rstd_ready=TT, x_ready=TT),
    "mix1": dict(turned0=TT + NTURNS1[0], turned1=TT + NTURNS1[1], free0=TT + NTURNS1[0],
                 free1=TT + NTURNS1[1], hi_part=2 * TT + 4, proj_copied=MIX1_PROJ - 1, rope_done=1, rotated=1,
                 scores=2 * 7, score_free=2 * 7, maxed=3, probs=3, mixed=3, ret_mixed=4, y_ready=4,
                 var_ready=TT, rstd_ready=TT, out_copied=TT, sink_sum=1, sink_exp=1, sum_ready=TT),
    "cond": dict(h_ready=TT),
    "mix2": dict(turned0=TT + NTURNS2[0], turned1=TT + NTURNS2[1], free0=TT + NTURNS2[0],
                 free1=TT + NTURNS2[1], hi_part=2 * TT + 4 + 6, proj_copied=MIX2_PROJ, rope_done=1,
                 scores=2 * 11, score_free=2 * 11, idx_summed=3, maxed=8, probs=8, mixed=8, out_copied=6,
                 squares=1, var_ready=1, rstd_ready=1, latent=TT, gates=1, y_ready=6, sum_ready=TT),
}
NAMES = sorted({n for s in SIGNALS.values() for n in s})
RING_USES = {"mix1": MIX1_PROJ + OUT_UNITS, "mix2": MIX2_PROJ + OUT_UNITS}


def signals_before(block, layer, position, name):
    total = lambda stages: sum(SIGNALS[s].get(name, 0) for s in stages)
    if block == 1:
        return layer * total(STAGES1) + total(STAGES1[:position])
    return DEPTH * total(STAGES1) + layer * total(STAGES2) + total(STAGES2[:position])


def slot_uses(stage, first):
    n = [0] * SLOTS
    if stage == "ffn":
        n[first] += ROUNDS + 1
        n[(first + 1) % SLOTS] += ROUNDS
        n[(first + 2) % SLOTS] += ROUNDS - 1
        return n, (first + 1) % SLOTS
    units = RING_USES.get(stage, 0)
    for m in range(units):
        n[(first + m) % SLOTS] += 1
    return n, (first + units) % SLOTS


def ring_plan(stages):
    plan, first, seen = [], 0, [0] * SLOTS
    for stage in stages:
        plan.append((first, list(seen)))
        uses, first = slot_uses(stage, first)
        seen = [a + b for a, b in zip(seen, uses)]
    assert first == 0, "a layer has to end where the next one begins"
    return plan, seen


RING1, LAYER_USES1 = ring_plan(STAGES1)
RING2, LAYER_USES2 = ring_plan(STAGES2)


class Stage:

    def __init__(self, block, layer, position):
        self.block, self.layer, self.position = block, layer, position
        self.first, self.seen = (RING1 if block == 1 else RING2)[position]

    def before(self, name):
        return signals_before(self.block, self.layer, self.position, name)

    def uses(self, slot):
        if self.block == 1:
            return self.layer * LAYER_USES1[slot] + self.seen[slot]
        return DEPTH * LAYER_USES1[slot] + self.layer * LAYER_USES2[slot] + self.seen[slot]

    def unit(self, m):
        slot = (self.first + m) % SLOTS
        return slot, self.uses(slot) + m // SLOTS


class Steps:

    def __init__(self, eng, sem, marks):
        self.eng, self.sem, self.marks, self.base, self.n = eng, sem, marks, 0, 0

    def wait(self, instruction):
        instruction.then_inc(self.sem, 1)
        self.n += 1
        self.eng.wait_ge(self.sem, self.base + self.n)

    def settle(self):
        self.eng.sem_inc(self.marks, 1)

    def loop(self, first, last, name):
        reg = self.eng.alloc_register(name)
        self.settle()
        self.eng.reg_mov(reg, self.eng.compute_val(self.base + self.n) if not isinstance(self.base, int)
                         else self.base + self.n)
        return _Loop(self, first, last, reg)


class _Loop:
    def __init__(self, steps, first, last, reg):
        self.steps, self.first, self.last, self.reg = steps, first, last, reg

    def __enter__(self):
        s = self.steps
        self.outer = (s.base, s.n)
        self.fori = s.eng.Fori(self.first, self.last)
        i = self.fori.__enter__()
        s.base, s.n = s.eng.snap(self.reg), 0
        return i

    def __exit__(self, *a):
        s = self.steps
        s.settle()
        s.eng.reg_add(self.reg, self.reg, s.n)
        self.fori.__exit__(*a)
        s.base, s.n = self.outer[0], self.outer[1] + (self.last - self.first) * s.n
        return False


T1_MASK, T1_DECAY, T1_ROPE, T1_RET = 0, 256, 256 + 2048, 256 + 2048 + 128
T1 = T1_RET + 128
T2_MASK, T2_B, T2_C, T2_ROPE = 0, 256, 256 + 6 * 256, 256 + 10 * 256
T2 = T2_ROPE + 64


def shape_tables():
    row, col = np.arange(P)[:, None], np.arange(2 * P)[None, :]
    back = row + P - col
    tab1, tab2 = np.zeros((P, T1), np.float64), np.zeros((P, T2), np.float64)
    tab1[:, T1_MASK:T1_DECAY] = np.where((back >= 0) & (back < P), 0.0, NEG)
    log_gamma = np.log1p(-np.exp2(-5.0 - np.arange(RET_HEADS)))
    for h in range(RET_HEADS):
        at = T1_DECAY + (h % 2 * 4 + h // 2) * 256
        tab1[:, at:at + 256] = np.where(col >= row, np.exp((col - row) * log_gamma[h]), 0.0) * HD ** -0.5
    pos = np.arange(S, dtype=np.float64)[:, None]

    def rotation(freqs):
        ang = (pos.astype(np.float32) * freqs.astype(np.float32)[None, :]).astype(np.float64)
        both = np.concatenate([np.cos(ang), np.sin(ang)], axis=1)
        return both.reshape(TT, P, -1).transpose(1, 0, 2).reshape(P, -1)

    tab1[:, T1_ROPE:T1_RET] = rotation(10000.0 ** (-np.arange(0, HD, 2) / HD))
    tab1[:, T1_RET:T1] = rotation(1.0 / (10000.0 ** np.linspace(0.0, 1.0, HD // 2)))
    tab2[:, T2_MASK:T2_B] = np.where(back >= 0, 0.0, NEG)
    slopes = 2.0 ** (-8.0 * np.arange(1, B_HEADS + C_HEADS + 1) / (B_HEADS + C_HEADS))
    times = ((back >= 0) & (back <= P)).astype(int) + ((back >= 0) & (back % 4 == 0)) + ((back >= 0) & (back % 16 == 0))
    log_times = np.where(times > 0, np.log(np.maximum(times, 1)), NEG)
    for h in range(B_HEADS):
        at = T2_B + (h % 2 * 3 + h // 2) * 256
        tab2[:, at:at + 256] = np.where(times > 0, log_times - slopes[h] * back, NEG)
    for h in range(C_HEADS):
        at = T2_C + (h % 2 * 2 + h // 2) * 256
        tab2[:, at:at + 256] = np.where(back >= 0, -slopes[B_HEADS + h] * back, NEG)
    tab2[:, T2_ROPE:T2] = rotation(10000.0 ** (-np.arange(0, A_ROPE, 2) / A_ROPE))
    return tab1.astype(np.float32), tab2.astype(np.float32), np.eye(P, dtype=np.float32)


def head_of(group, pair, half):
    return pair + 4 * half if group == "W" else 2 * pair + half


def build(nc, t, out):
    with ExitStack() as ctx:
        def sb(name, shape, dt=F32):
            return ctx.enter_context(nc.sbuf_tensor(name, shape, dt))

        def sem(name):
            return ctx.enter_context(nc.semaphore(name))

        raw = [sb(f"w_raw{j}", [P, UNIT]) for j in range(SLOTS)]
        w_hi = [sb(f"w_hi{j}", [P, UNIT], F32R) for j in range(SLOTS)]
        w_lo = [sb(f"w_lo{j}", [P, UNIT], F32R) for j in range(SLOTS)]
        x = sb("x", [P, TT, D])
        y = sb("y", [P, TT, D])
        col_hi = sb("col_hi", [P, KT, S], F32R)
        col_lo = sb("col_lo", [P, KT, S], F32R)
        lat_hi = sb("lat_hi", [P, KT, S], F32R)
        lat_lo = sb("lat_lo", [P, KT, S], F32R)
        arena = sb("arena", [P, 10880])
        score = sb("score", [P, 2, HALF])
        prob = sb("prob", [P, 2, HALF])
        prob_t = sb("prob_t", [P, 2, HALF])
        table = sb("table", [P, max(T1, T2)])
        ident = sb("ident", [P, P])
        ones = sb("ones", [P, P])
        norm_g = sb("norm_g", [P, D])
        norm_b = sb("norm_b", [P, D])
        mod = sb("mod", [P, MOD])
        small = sb("small", [P, 280])

        silu_a, hidden = arena[:, 0:HALF], arena[:, HALF:2 * HALF]
        rows1 = arena[:, 0:TT * IN1].rearrange("p (t n) -> p t n", t=TT)
        o = TT * IN1
        q1_t = arena[:, o:o + 1024].rearrange("p (j s) -> p j s", j=4)
        k1_t = arena[:, o + 1024:o + 1280]
        qr_t = arena[:, o + 1280:o + 2304].rearrange("p (j s) -> p j s", j=4)
        kr_t = arena[:, o + 2304:o + 3328].rearrange("p (j s) -> p j s", j=4)
        rot_tmp = arena[:, o + 3328:o + 4352]
        rows2 = arena[:, 0:TT * R_ROW].rearrange("p (t n) -> p t n", t=TT)
        o = TT * R_ROW
        cols2 = arena[:, o:o + C_TILES * S].rearrange("p (j s) -> p j s", j=C_TILES)
        ka = arena[:, o:o + TT * A_HEADS * A_HD].rearrange("p (t h d) -> p t h d", t=TT, h=A_HEADS)
        qa_t = arena[:, o + C_QKB * S:o + C_QKC * S].rearrange("p (h s) -> p h s", h=A_HEADS)
        ka_t = mod[:, 0:A_HEADS * S].rearrange("p (h s) -> p h s", h=A_HEADS)
        o += C_TILES * S
        idx_score = arena[:, o:o + 512].rearrange("p (t s) -> p t s", t=TT)
        not_taken = arena[:, o + 512:o + 1024].rearrange("p (t s) -> p t s", t=TT)
        rope_tmp = arena[:, o + 1024:o + 1536]
        ada_w = mod[:, 0:KT * MOD_W].rearrange("p (k n) -> p k n", k=KT)
        ada_sum = mod[:, KT * MOD_W:(KT + 1) * MOD_W]
        ada_row = mod[0:1, (KT + 1) * MOD_W:(KT + 2) * MOD_W]
        ada_bias = mod[0:1, (KT + 2) * MOD_W:(KT + 3) * MOD_W]
        mod_rows = nc.dram_tensor("mod_rows", (DEPTH, MOD), F32, kind="Internal").ap()

        at = [0]

        def few(n):
            at[0] += n
            assert at[0] <= small.shape[1]
            return small[:, at[0] - n:at[0]]
        stats = few(TT * 12).rearrange("p (t a b) -> p t a b", t=TT, a=2)
        mean_var = few(TT * 2).rearrange("p (t a) -> p t a", t=TT)
        rstd = few(TT)
        gn_sum = few(TT * 8).rearrange("p (t h) -> p t h", t=TT)
        gn_var = few(TT * 8).rearrange("p (t h) -> p t h", t=TT)
        gn_rstd = few(TT * 8).rearrange("p (t h) -> p t h", t=TT)
        lat_var = few(TT * 2).rearrange("p (a t) -> p a t", a=2)
        lat_rstd = few(TT * 2).rearrange("p (a t) -> p a t", a=2)
        row_max = few(TT * 8).rearrange("p (t h) -> p t h", t=TT)
        neg_max = few(TT * 8).rearrange("p (t h) -> p t h", t=TT)
        row_sum = few(TT * 8).rearrange("p (t h) -> p t h", t=TT)
        row_inv = few(TT * 8).rearrange("p (t h) -> p t h", t=TT)
        sink_e = few(TT * 8).rearrange("p (t h) -> p t h", t=TT)
        sinks = few(8)
        top8 = few(8)
        idx_w = few(TT * 8).rearrange("p (t h) -> p t h", t=TT)
        c_raw = few(KT)
        c_silu = few(KT)
        minus_half = few(8)

        ps = ctx.enter_context(nc.psum_tensor("ps", [P, 8, HALF], F32))

        landed = [sem(f"w_landed{j}") for j in range(SLOTS)]
        hi_ready = [sem(f"w_hi_ready{j}") for j in range(SLOTS)]
        lo_ready = [sem(f"w_lo_ready{j}") for j in range(SLOTS)]
        used = [sem(f"w_used{j}") for j in range(SLOTS)]
        k_piece, w_piece = sem("k_piece_landed"), sem("w_piece_landed")
        sg = {n: sem(n) for n in NAMES}
        x_landed, tables_in, ident_in = sem("x_landed"), sem("tables_landed"), sem("ident_landed")
        params_in, sinks_in, lat_g_in, mod_in, gate_in, c_in, ada_in, ada_bias_in, mod_stored = (
            sem(n) for n in ("norm_params_landed", "sinks_landed", "latent_gains_landed", "shift_scale_landed",
                             "gate_landed", "c_landed", "ada_chunk_landed", "ada_bias_landed", "mod_stored"))
        const_ready, c_ready, out_landed = sem("const_ready"), sem("c_ready"), sem("out_landed")
        v_steps, a_steps, g_steps, p_marks, s_marks, a_marks, v_marks, t_marks = (
            sem(n) for n in ("vector_steps", "scalar_steps", "gpsimd_steps", "gpsimd_marks", "sync_marks",
                             "scalar_marks", "vector_marks", "tensor_marks"))
        turned, free = [sg["turned0"], sg["turned1"]], [sg["free0"], sg["free1"]]
        free_name = ["free0", "free1"]

        def bank(b, n=HALF):
            return ps[:, b, 0:n]

        def by_pair(tile, t_, group, pairs):
            if group == "W":
                v = tile[:, t_, :].rearrange("p (f j) -> p f j", f=2)
            else:
                v = tile[:, t_, :].rearrange("p (j f) -> p f j", f=2)
            return v[:, :, pairs[0]:pairs[-1] + 1]

        def group_heads(group):
            return {"W": 8, "A": 6, "B": 6, "C": 4}[group]

        steps_of = lambda group: STEPS1 if group == "W" else STEPS2[group]
        ORDER2 = {("B", 0): 0, ("B", 1): 1, ("B", 2): 2, ("C", 0): 3, ("C", 1): 4,
                  ("A", 0): 5, ("A", 1): 6, ("A", 2): 7}

        def ordinal(group, s):
            return s if group == "W" else ORDER2[group, s]

        def scored_before(group, s):
            return s if group == "W" else 3 + ORDER2[group, s]

        block = ctx.enter_context(nc.Block())

        @block.sync
        def _(sp):
            def settle():
                sp.sem_inc(s_marks, 1)

            def load(slot, use, dst, src, extra=()):
                sp.wait_ge(hi_ready[slot], use + 1)
                settle()
                sp.wait_ge(lo_ready[slot], use + 1)
                settle()
                sp.dma_start(dst, src).then_inc(landed[slot], 16)
                for d, s_, signal in extra:
                    sp.dma_start(d, s_).then_inc(signal, 16)

            def rows_of(slot, k, n):
                return raw[slot][:, 0:k * n].rearrange("p (k n) -> p k n", k=k)

            def ffn(st, l, gate_up, down):
                g, u, d = st.first, (st.first + 1) % SLOTS, (st.first + 2) % SLOTS
                def gu(i, slot, first_col):
                    load(slot, st.uses(slot) + i, rows_of(slot, KT, FU),
                         gate_up[l, :, bass.ds(first_col + i * FU, FU)].rearrange("(k p) n -> p k n", p=P))

                def dn(i, slot, use):
                    load(slot, use, rows_of(slot, 2, D),
                         down[l, bass.ds(i * FU, FU), :].rearrange("(k p) n -> p k n", p=P))
                for i in range(2):
                    gu(i, g, 0)
                    gu(i, u, F)
                with sp.Fori(1, ROUNDS - 1) as i:
                    dn(i - 1, d, st.uses(d) + i - 1)
                    gu(i + 1, g, 0)
                    gu(i + 1, u, F)
                dn(ROUNDS - 2, d, st.uses(d) + ROUNDS - 2)
                dn(ROUNDS - 1, g, st.uses(g) + ROUNDS)

            def out_units(st, l, first, w):
                for i in range(OUT_UNITS):
                    slot, use = st.unit(first + i)
                    load(slot, use, rows_of(slot, 2, D),
                         w[l, i * 2 * P:(i + 1) * 2 * P, :].rearrange("(k p) n -> p k n", p=P))

            with sp.Fori(0, DEPTH) as l:
                for pos, name in enumerate(STAGES1):
                    st = Stage(1, l, pos)
                    if name == "ffn":
                        n = 1 if pos == 0 else 2
                        ffn(st, l, t[f"ffn{n}_w_gu"], t[f"ffn{n}_w_down"])
                    if name == "mix1":
                        for m, (c, w) in enumerate(MIX1_COLS):
                            slot, use = st.unit(m)
                            half = m - (MIX1_PROJ - 2)
                            k0, k1 = (half * HALF_KT, (half + 1) * HALF_KT) if half >= 0 else (0, KT)
                            load(slot, use, rows_of(slot, k1 - k0, w),
                                 t["w_in"][l, k0 * P:k1 * P, c:c + w].rearrange("(k p) n -> p k n", p=P))
                        out_units(st, l, MIX1_PROJ, t["w_out"])
            with sp.Fori(0, DEPTH) as l:
                st = Stage(2, l, 1)
                for m, unit in enumerate(MIX2_UNITS):
                    slot, use = st.unit(m)
                    if unit[0] in ("T", "N"):
                        width = sum(w for _, w in unit[1])
                        dst, c0, parts = rows_of(slot, KT, width), 0, []
                        for c, w in unit[1]:
                            parts.append((dst[:, :, c0:c0 + w],
                                          t["w_in_2"][l, :, c:c + w].rearrange("(k p) n -> p k n", p=P)))
                            c0 += w
                        signal = k_piece if unit[1][0][0] == KI else w_piece
                        load(slot, use, *parts[0], extra=[(d, s_, signal) for d, s_ in parts[1:]])
                    else:
                        w = {"UQ": t["w_uq_2"], "UK": t["w_uk_2"], "UV": t["w_uv_2"]}[unit[0]]
                        k = (Q_LORA if unit[0] == "UQ" else KV_LORA) // P
                        load(slot, use, rows_of(slot, k, 192),
                             w[l, :, unit[1] * 192:(unit[1] + 1) * 192].rearrange("(k p) n -> p k n", p=P))
                out_units(st, l, MIX2_PROJ, t["w_out_2"])
            sp.wait_ge(sg["x_ready"], TT + signals_before(2, DEPTH, 0, "x_ready"))
            sp.dma_start(out[0].rearrange("(t p) d -> p t d", p=P), x[:, :, :]).then_inc(out_landed, 16)
            sp.wait_ge(out_landed, 16)

        @block.tensor
        def _(pe):
            def unit_ready(slot, use):
                pe.wait_ge(hi_ready[slot], use + 2)
                pe.wait_ge(lo_ready[slot], use + 2)

            def three(dst, a_hi, a_lo, b_hi, b_lo, start, stop):
                pe.matmul(dst, a_hi, b_hi, start=start, stop=False)
                pe.matmul(dst, a_hi, b_lo, start=False, stop=False)
                return pe.matmul(dst, a_lo, b_hi, start=False, stop=stop)

            def keep_warm(ns, b):
                for _ in range(round(ns / 213)):
                    pe.matmul(bank(b, P), ident[:, :], ident[:, :], start=True, stop=True)

            def turned_unit(slot, b, width, tiles=range(TT), between=None):
                hi = w_hi[slot][:, 0:KT * width].rearrange("p (k n) -> p k n", k=KT)
                lo = w_lo[slot][:, 0:KT * width].rearrange("p (k n) -> p k n", k=KT)
                toks = slice(tiles[0] * P, (tiles[-1] + 1) * P)
                for n in range(width // P):
                    for k in range(KT):
                        last = three(ps[:, b, n * S + toks.start:n * S + toks.stop], hi[:, k, n * P:(n + 1) * P],
                                     lo[:, k, n * P:(n + 1) * P], col_hi[:, k, toks], col_lo[:, k, toks],
                                     k == 0, k == KT - 1)
                    if n == 0 and between is not None:
                        between()
                if tiles[-1] == TT - 1:
                    last.then_inc(used[slot], 1)

            def row_unit(slot, b, width, a_hi, a_lo, kts, tiles=range(TT), between=None):
                hi = w_hi[slot][:, 0:len(kts) * width].rearrange("p (k n) -> p k n", k=len(kts))
                lo = w_lo[slot][:, 0:len(kts) * width].rearrange("p (k n) -> p k n", k=len(kts))
                for i in tiles:
                    tok = slice(i * P, (i + 1) * P)
                    for k, kk in enumerate(kts):
                        last = three(ps[:, b, i * 256:i * 256 + width], a_hi[:, kk, tok], a_lo[:, kk, tok],
                                     hi[:, k, :], lo[:, k, :], k == 0, k == len(kts) - 1)
                        if k == 3 and between is not None:
                            between()
                if tiles[-1] == TT - 1:
                    last.then_inc(used[slot], 1)

            def half_unit(slot, half):
                hi = w_hi[slot][:, 0:HALF_KT * 256].rearrange("p (k n) -> p k n", k=HALF_KT)
                lo = w_lo[slot][:, 0:HALF_KT * 256].rearrange("p (k n) -> p k n", k=HALF_KT)
                for i in range(TT):
                    tok = slice(i * P, (i + 1) * P)
                    for k in range(HALF_KT):
                        kk = half * HALF_KT + k
                        last = three(bank(4 + i, 256), col_hi[:, kk, tok], col_lo[:, kk, tok], hi[:, k, :], lo[:, k, :],
                                     kk == 0, kk == KT - 1)
                last.then_inc(used[slot], 1)

            def wide_unit(slot, banks, a_hi, a_lo, kts, start, stop, tiles=range(TT)):
                hi = w_hi[slot][:, :].rearrange("p (k n) -> p k n", k=2)
                lo = w_lo[slot][:, :].rearrange("p (k n) -> p k n", k=2)
                for i in tiles:
                    for n in range(2):
                        for k, kk in enumerate(kts):
                            cols = slice(n * HALF, (n + 1) * HALF)
                            last = three(bank(banks[i] + n), a_hi[:, kk, i * P:(i + 1) * P],
                                         a_lo[:, kk, i * P:(i + 1) * P], hi[:, k, cols], lo[:, k, cols],
                                         start and k == 0, stop and k == 1)
                return last

            def finish_sums(st, units, banks):
                for i in range(TT):
                    for n, (slot, a_hi, a_lo, kts, waits) in enumerate(units):
                        if i == 0:
                            waits()
                        last = wide_unit(slot, banks, a_hi, a_lo, kts, False, n == 1, tiles=[i])
                        if n == 0 and i == TT - 1:
                            last.then_inc(used[slot], 1)
                    last.then_inc(sg["sum_ready"], 1)
                pe.wait_ge(sg["sum_ready"], st.before("sum_ready") + TT)
                pe.sem_inc(used[units[1][0]], 1)

            def turn_rows(st, src, wait_name, wait_base, i):
                pe.wait_ge(sg[wait_name], wait_base + i + 1)
                for hf in range(2):
                    pe.wait_ge(free[hf], st.before(free_name[hf]) + i + 1)
                    for k in range(4):
                        last = pe.transpose(ps[:, 6 + hf, k * P:(k + 1) * P],
                                            src[:, i, (4 * hf + k) * P:(4 * hf + k + 1) * P], ident[:, :])
                    last.then_inc(turned[hf], 1)

            def start_stage(st, src, wait_name, wait_base, first_unit, idle):
                keep_warm(idle[0], 7)
                turn_rows(st, src, wait_name, wait_base, 0)
                keep_warm(idle[1], 5)
                for hf in range(2):
                    pe.wait_ge(free[hf], st.before(free_name[hf]) + 2)
                unit_ready(*st.unit(0))
                first_unit([0], lambda: turn_rows(st, src, wait_name, wait_base, 1))
                for hf in range(2):
                    pe.wait_ge(free[hf], st.before(free_name[hf]) + TT + 1)
                first_unit([1], None)

            def ffn(st):
                g, u, d = st.first, (st.first + 1) % SLOTS, (st.first + 2) % SLOTS
                h_hi = lambda s_: lat_hi[:, 2 * s_:2 * s_ + 2, :]
                h_lo = lambda s_: lat_lo[:, 2 * s_:2 * s_ + 2, :]

                start_stage(st, x, "x_ready", st.before("x_ready"),
                            lambda tiles, between: turned_unit(g, 4, FU, tiles, between),
                            (0, IDLE_OPEN) if st.position == 0 else (0, IDLE_IN))

                def gate(i):
                    unit_ready(g, st.uses(g) + i)
                    turned_unit(g, 4, FU)

                def up(i):
                    unit_ready(u, st.uses(u) + i)
                    turned_unit(u, 5, FU)

                def down_ready(i, slot, use):
                    unit_ready(slot, use)
                    pe.wait_ge(sg["h_lo"], st.before("h_lo") + i + 1)

                def down(i, start=False):
                    down_ready(i, d, st.uses(d) + i)
                    wide_unit(d, (0, 2), h_hi(0), h_lo(0), (0, 1), start, False).then_inc(used[d], 1)

                up(0)
                pe.wait_ge(sg["silu_done"], st.before("silu_done") + 1)
                gate(1)
                pe.wait_ge(sg["h_done"], st.before("h_done") + 1)
                up(1)
                down(0, start=True)
                with pe.Fori(2, ROUNDS - 1) as i:
                    pe.wait_ge(sg["silu_done"], st.before("silu_done") + i)
                    gate(i)
                    pe.wait_ge(sg["h_done"], st.before("h_done") + i)
                    up(i)
                    pe.wait_ge(sg["mod_summed"], st.before("mod_summed") + i - 1)
                    pe.matmul(bank(6, MOD_W), ones[:, :], ada_sum, start=True, stop=True)\
                        .then_inc(sg["mod_spread"], 1)
                    down(i - 1)
                i = ROUNDS - 1
                pe.wait_ge(sg["silu_done"], st.before("silu_done") + i)
                gate(i)
                pe.wait_ge(sg["h_done"], st.before("h_done") + i)
                up(i)
                finish_sums(st, [(d, h_hi(0), h_lo(0), (0, 1), lambda: down_ready(i - 1, d, st.uses(d) + i - 1)),
                             (g, h_hi(1), h_lo(1), (0, 1), lambda: down_ready(i, g, st.uses(g) + ROUNDS))], (0, 2))

            def turn_banks(st, turns, job, tiles, which=0):
                b, n = turns[job][which]
                pe.wait_ge(free[b], st.before(free_name[b]) + TT + n + 1)
                for src, c in tiles:
                    width = math.prod(src.shape[1:])
                    last = pe.transpose(ps[0:width, 6 + b, c:c + P], src, ident[:, :])
                last.then_inc(turned[b], 1)

            def scores_free(st, before):
                if before:
                    pe.wait_ge(sg["score_free"], st.before("score_free") + 2 * before)

            def attend_scores(st, group, s):
                _, i, pairs = steps_of(group)[s]
                scores_free(st, scored_before(group, s))
                keys = (i + 1) * P
                for half in range(2):
                    for n, j in enumerate(pairs):
                        rows = slice(64 * half, 64 * half + 64)
                        toks = slice(i * P, (i + 1) * P)
                        if group == "W":
                            q, k = q1_t[rows, j, toks], k1_t[rows, 0:keys]
                        elif group == "B":
                            q, k = cols2[rows, C_QKB + j, toks], cols2[rows, C_QKB + 3 + j, 0:keys]
                        elif group == "C":
                            q, k = cols2[rows, C_QKC + j, toks], cols2[rows, C_QKC + 2 + j, 0:keys]
                        else:
                            q, k = qa_t[0:A_HD, 2 * j + half, toks], ka_t[0:A_HD, 2 * j + half, 0:keys]
                        last = pe.matmul(ps[:, half, n * keys:(n + 1) * keys], q, k, start=True, stop=True)
                    last.then_inc(sg["scores"], 1)

            def attend_turn(st, turns, group, s):
                job = ("turn", s) if group == "W" else ("turn", group, s)
                _, i, pairs = steps_of(group)[s]
                pe.wait_ge(sg["probs"], st.before("probs") + ordinal(group, s) + 1)
                for half in range(2):
                    n = len(pairs) * (i + 1)
                    turn_banks(st, turns, job, [(prob[:, half, c * P:(c + 1) * P], c * P) for c in range(n)], half)

            def attend_mix(st, turns, group, s):
                job = ("turn", s) if group == "W" else ("turn", group, s)
                _, i, pairs = steps_of(group)[s]
                for half in range(2):
                    b, n = turns[job][half]
                    pe.wait_ge(free[b], st.before(free_name[b]) + TT + n + 2)
                if group in "AC" and s == 0:
                    pe.wait_ge(sg["out_copied"], st.before("out_copied") + (2 if group == "C" else 4))
                if (group, s) == ("A", 0):
                    pe.wait_ge(sg["proj_copied"], st.before("proj_copied") + UNITS_UV)
                for half in range(2):
                    for n, j in enumerate(pairs):
                        h = head_of(group, j, half)
                        for k in range(i + 1):
                            v = {"W": rows1[:, k, VA + half * HD:VA + half * HD + HD] if group == "W" else None,
                                 "A": rows2[:, k, R_VA + h * HD:R_VA + h * HD + HD],
                                 "B": rows2[:, k, R_VB + h * HD:R_VB + h * HD + HD],
                                 "C": rows2[:, k, R_VC + h % 4 * HD:R_VC + h % 4 * HD + HD]}[group]
                            c = (n * (i + 1) + k) * P
                            last = pe.matmul(ps[:, 2 + i, h * HD:(h + 1) * HD], prob_t[:, half, c:c + P], v,
                                             start=k == 0, stop=k == i)
                last.then_inc(sg["mixed"], 1)

            def y_turn(st, turns, job, parts):
                _, i, part = job
                order = [j for j in (MIX1_WALK if st.block == 1 else MIX2_WALK) if j[0] == "ycols"].index(job)
                pe.wait_ge(sg["y_ready"], st.before("y_ready") + order + 1)
                turn_banks(st, turns, job, [(y[:, i, k * P:(k + 1) * P], n * P)
                                            for n, k in enumerate(parts[part])])

            def out_unit(st, turns, i, first, parts, scored, copies):
                def ready(i):
                    unit_ready(*st.unit(first + i))
                    for part, tiles in enumerate(parts):
                        if {2 * i, 2 * i + 1} & set(tiles):
                            for tok in range(TT):
                                b, n = turns["ycols", tok, part][0]
                                pe.wait_ge(free[b], st.before(free_name[b]) + TT + n + 2)

                if i < OUT_UNITS - 2:
                    ready(i)
                    if i == 0:
                        scores_free(st, scored)
                        pe.wait_ge(sg["proj_copied"], st.before("proj_copied") + copies)
                    slot = st.unit(first + i)[0]
                    wide_unit(slot, (4, 0), col_hi, col_lo, (2 * i, 2 * i + 1), i == 0, False)\
                        .then_inc(used[slot], 1)
                elif i == OUT_UNITS - 1:
                    finish_sums(st, [(st.unit(first + n)[0], col_hi, col_lo, (2 * n, 2 * n + 1), lambda n=n: ready(n))
                                 for n in (i - 1, i)], (4, 0))

            def mix1(st):
                slot = st.unit(0)[0]
                start_stage(st, x, "x_ready", st.before("x_ready"),
                            lambda tiles, between: row_unit(slot, 4, MIX1_COLS[0][1], col_hi, col_lo, range(KT),
                                                            tiles, between), (0, IDLE_IN))
                for job in MIX1_WALK[1:]:
                    if job[0] == "unit":
                        m = job[1]
                        slot, use = st.unit(m)
                        unit_ready(slot, use)
                        if m >= 2:
                            pe.wait_ge(sg["proj_copied"], st.before("proj_copied") + min(m - 1, MIX1_PROJ - 3))
                        if m < MIX1_PROJ - 2:
                            row_unit(slot, 4 + m % 2, MIX1_COLS[m][1], col_hi, col_lo, range(KT))
                        else:
                            if m == MIX1_PROJ - 2:
                                pe.wait_ge(sg["proj_copied"], st.before("proj_copied") + m)
                            half_unit(slot, m - (MIX1_PROJ - 2))
                    elif job[0] == "trqk":
                        pe.wait_ge(sg["rope_done"], st.before("rope_done") + 1)
                        for i in range(TT):
                            turn_banks(st, TURNS1, job, [(rows1[:, i, QA + j * P:QA + (j + 1) * P], j * P)
                                                         for j in range(4)], i)
                        turn_banks(st, TURNS1, job, [(rows1[:, i, KA:VA], i * P) for i in range(TT)], 2)
                    elif job[0] == "score":
                        if job[1] == 0:
                            for which in range(3):
                                b, n = TURNS1["trqk",][which]
                                pe.wait_ge(free[b], st.before(free_name[b]) + TT + n + 2)
                        attend_scores(st, "W", job[1])
                    elif job[0] == "turn":
                        attend_turn(st, TURNS1, "W", job[1])
                    elif job[0] == "mix":
                        attend_mix(st, TURNS1, "W", job[1])
                    elif job[0] == "trret":
                        if job[1] == 0:
                            pe.wait_ge(sg["rotated"], st.before("rotated") + 1)
                        c, i = (QR, KR)[job[1] // 2], job[1] % 2
                        turn_banks(st, TURNS1, job, [(rows1[:, i, c + j * P:c + (j + 1) * P], j * P) for j in range(4)])
                    elif job[0] == "ret":
                        j = job[1]
                        if j == 0:
                            for b in range(2):
                                n = TURNS1["trret", 2 + b][0][1]
                                pe.wait_ge(free[b], st.before(free_name[b]) + TT + n + 2)
                        scores_free(st, 3 + j)
                        for half in range(2):
                            rows = slice(64 * half, 64 * half + 64)
                            pe.matmul(ps[:, half, 0:S], kr_t[rows, j, 0:P], qr_t[rows, j, :], start=True, stop=True)
                            pe.matmul(ps[:, half, S:S + P], kr_t[rows, j, P:S], qr_t[rows, j, P:S],
                                      start=True, stop=True).then_inc(sg["scores"], 1)
                    elif job[0] == "retmix":
                        j = job[1]
                        if j == 0:
                            keep_warm(IDLE_RETMIX, 7)
                            pe.wait_ge(sg["out_copied"], st.before("out_copied") + TT)
                        pe.wait_ge(sg["score_free"], st.before("score_free") + 2 * (4 + j))
                        decayed = prob if j % 2 == 0 else score
                        for half in range(2):
                            h = 2 * j + half
                            v = lambda k: rows1[:, k, VR + h * HD:VR + (h + 1) * HD]
                            o_ = slice(h * HD, (h + 1) * HD)
                            pe.matmul(ps[:, 2, o_], decayed[:, half, 0:P], v(0), start=True, stop=True)
                            pe.matmul(ps[:, 3, o_], decayed[:, half, P:S], v(0), start=True, stop=False)
                            last = pe.matmul(ps[:, 3, o_], decayed[:, half, S:S + P], v(1), start=False, stop=True)
                        last.then_inc(sg["ret_mixed"], 1)
                    elif job[0] == "ycols":
                        y_turn(st, TURNS1, job, YPARTS1)
                    elif job[0] == "out":
                        out_unit(st, TURNS1, job[1], MIX1_PROJ, YPARTS1, 7, MIX1_PROJ - 1)

            def mix2(st):
                slot = st.unit(0)[0]
                start_stage(st, y, "h_ready", st.before("h_ready") - TT,
                            lambda tiles, between: turned_unit(slot, 4, 256, tiles, between),
                            (IDLE_COND, IDLE_COND_SPLIT))
                for job in MIX2_WALK[1:]:
                    if job[0] == "unit":
                        m = job[1]
                        unit = MIX2_UNITS[m]
                        slot, use = st.unit(m)
                        unit_ready(slot, use)
                        if m >= 2:
                            pe.wait_ge(sg["proj_copied"], st.before("proj_copied") + m - 1)
                        if unit[0] == "T":
                            turned_unit(slot, 4 + m % 2, sum(w for _, w in unit[1]))
                        elif unit[0] == "N":
                            row_unit(slot, 4 + m % 2, sum(w for _, w in unit[1]), col_hi, col_lo, range(KT))
                        else:
                            if unit == ("UQ", 0):
                                for g in range(2, 4):
                                    b, n = TURNS2["trlat", g][0]
                                    pe.wait_ge(free[b], st.before(free_name[b]) + TT + n + 2)
                            row_unit(slot, 4 + m % 2, 192, lat_hi, lat_lo,
                                     range(6) if unit[0] == "UQ" else range(6, 8))
                    elif job[0] == "idx":
                        i, pairs = IDX_STEPS[job[1]]
                        if job[1] == 0:
                            pe.wait_ge(sg["proj_copied"], st.before("proj_copied") + 3)
                        scores_free(st, job[1])
                        keys = (i + 1) * P
                        for half in range(2):
                            rows = slice(64 * half, 64 * half + 64)
                            for n, j in enumerate(pairs):
                                last = pe.matmul(ps[:, half, n * keys:(n + 1) * keys],
                                                 cols2[rows, C_QI + j, i * P:(i + 1) * P],
                                                 cols2[rows, C_KI, 0:keys], start=True, stop=True)
                            last.then_inc(sg["scores"], 1)
                    elif job[0] == "trlat":
                        i, hf = job[1] // 2, job[1] % 2
                        pe.wait_ge(sg["latent"], st.before("latent") + i + 1)
                        turn_banks(st, TURNS2, job, [(rows2[:, i, (4 * hf + k) * P:(4 * hf + k + 1) * P], k * P)
                                                     for k in range(4)])
                    elif job[0] == "trA":
                        g = job[1]
                        if g == 0:
                            pe.wait_ge(sg["rope_done"], st.before("rope_done") + 1)
                        if g == 3:
                            pe.wait_ge(sg["proj_copied"], st.before("proj_copied") + UNITS_UK)
                        tiles = []
                        for n in range(2):
                            for i in range(TT):
                                h = 2 * (g % 3) + n
                                src = (rows2[:, i, R_QA + h * A_HD:R_QA + (h + 1) * A_HD] if g < 3
                                       else ka[:, i, h, :])
                                tiles.append((src, (n * TT + i) * P))
                        turn_banks(st, TURNS2, job, tiles)
                    elif job[0] == "score":
                        group, s = job[1:]
                        if s == 0:
                            if group == "A":
                                for g in range(4, 6):
                                    b, n = TURNS2["trA", g][0]
                                    pe.wait_ge(free[b], st.before(free_name[b]) + TT + n + 2)
                            else:
                                pe.wait_ge(sg["proj_copied"],
                                           st.before("proj_copied") + {"B": UNITS_B, "C": UNITS_C}[group])
                        attend_scores(st, group, s)
                    elif job[0] == "turn":
                        attend_turn(st, TURNS2, *job[1:])
                    elif job[0] == "mix":
                        attend_mix(st, TURNS2, *job[1:])
                    elif job[0] == "ycols":
                        if job[1:] == (0, 0):
                            pe.wait_ge(sg["proj_copied"], st.before("proj_copied") + MIX2_PROJ)
                            keep_warm(IDLE_GATED, 4)
                        y_turn(st, TURNS2, job, YPARTS2)
                    elif job[0] == "out":
                        out_unit(st, TURNS2, job[1], MIX2_PROJ, YPARTS2, 11, MIX2_PROJ)

            for j in range(SLOTS):
                pe.sem_inc(used[j], 1)
            pe.wait_ge(ident_in, 16)
            keep_warm(IDLE_START, 7)
            with pe.Fori(0, DEPTH) as l:
                for pos, name in enumerate(STAGES1):
                    st = Stage(1, l, pos)
                    if name == "ffn":
                        ffn(st)
                    if name == "mix1":
                        mix1(st)
            with pe.Fori(0, DEPTH) as l:
                mix2(Stage(2, l, 1))

        @block.scalar
        def _(act):
            steps = Steps(act, a_steps, a_marks)

            def split(slot, use, n=UNIT, piece=None):
                act.wait_ge(landed[slot], 16 * (use + 1))
                if piece is not None:
                    act.wait_ge(*piece)
                act.wait_ge(used[slot], use + 1)
                act.activation(w_hi[slot][:, 0:n], raw[slot][:, 0:n], ACT.Copy).then_inc(hi_ready[slot], 1)

            def split_unit(st, m, sizes, piece_of=lambda m: None):
                if m < len(sizes):
                    split(*st.unit(m), sizes[m], piece_of(m))
                elif m == len(sizes) and st.block == 1:
                    split(*st.unit(m))

            def cols_hi(st, i, hf, dst, nth):
                act.wait_ge(turned[hf], st.before(f"turned{hf}") + i + 1)
                act.activation(dst[:, 4 * hf:4 * hf + 4, i * P:(i + 1) * P],
                               bank(6 + hf).rearrange("p (k s) -> p k s", k=4), ACT.Copy)\
                   .then_inc(sg["hi_part"], 1)

            def rows_hi(st, use_of_1=None):
                if st.position in (0, 1) and st.block * st.position != 1:
                    split(*st.unit(0))
                for i in range(TT):
                    for hf in range(2):
                        cols_hi(st, i, hf, col_hi, 2 * i + hf)
                    if i == 0:
                        split(*st.unit(1))

            def turn_wait(st, turns, job, which=0):
                b, n = turns[job][which]
                act.wait_ge(turned[b], st.before(f"turned{b}") + TT + n + 1)
                return b

            def turn_copy(st, turns, job, dst, src_n, which=0, rows=P):
                b = turn_wait(st, turns, job, which)
                act.activation(dst, ps[0:rows, 6 + b, 0:src_n], ACT.Copy).then_inc(free[b], 1)

            def attend_probs(st, group, s, turns):
                _, i, pairs = steps_of(group)[s]
                o_ = ordinal(group, s)
                act.wait_ge(sg["maxed"], st.before("maxed") + o_ + 1)
                if o_ > 0:
                    before = [("turn", s - 1)] if group == "W" else [("turn", g, n) for (g, n), v in ORDER2.items()
                                                                     if v == o_ - 1]
                    for half in range(2):
                        b, n = turns[before[0]][half]
                        act.wait_ge(turned[b], st.before(f"turned{b}") + TT + n + 1)
                keys = (i + 1) * P
                for half in range(2):
                    for n, j in enumerate(pairs):
                        h = head_of(group, j, half)
                        last = act.activation(prob[:, half, n * keys:(n + 1) * keys],
                                              score[:, half, n * keys:(n + 1) * keys], ACT.Exp,
                                              bias=neg_max[:, i, h:h + 1], accum_out=row_sum[:, i, h:h + 1])
                last.then_inc(sg["probs"], 1)

            def attend_copy(st, turns, group, s):
                job = ("turn", s) if group == "W" else ("turn", group, s)
                _, i, pairs = steps_of(group)[s]
                o_ = ordinal(group, s)
                if o_ > 0:
                    act.wait_ge(sg["mixed"], st.before("mixed") + o_)
                n = len(pairs) * (i + 1) * P
                for half in range(2):
                    turn_copy(st, turns, job, prob_t[:, half, 0:n], n, half)

            def y_hi(st, turns, job, parts):
                _, i, part = job
                tiles = parts[part]
                turn_wait(st, turns, job)
                act.activation(col_hi[:, tiles[0]:tiles[-1] + 1, i * P:(i + 1) * P],
                               bank(6 + i, len(tiles) * P).rearrange("p (k s) -> p k s", s=P), ACT.Copy)\
                   .then_inc(sg["hi_part"], 1)

            def ffn(st, last_stage=False):
                g, u, d = st.first, (st.first + 1) % SLOTS, (st.first + 2) % SLOTS
                rows_hi(st)

                def silu(i):
                    act.wait_ge(used[g], st.uses(g) + i + 2)
                    if not isinstance(i, int) or i > 0:
                        act.wait_ge(sg["h_done"], st.before("h_done") + i)
                    act.activation(silu_a, bank(4), ACT.Silu).then_inc(sg["silu_done"], 1)

                def h_hi(i, s_):
                    act.wait_ge(sg["h_done"], st.before("h_done") + i + 1)
                    if s_ == 0 and (not isinstance(i, int) or i > 0):
                        act.wait_ge(used[d], st.uses(d) + i + 1)
                    act.activation(lat_hi[:, 2 * s_:2 * s_ + 2, :].rearrange("p a b -> p (a b)"), hidden, ACT.Copy)\
                       .then_inc(sg["h_hi"], 1)

                silu(0)
                split(g, st.uses(g) + 1)
                split(u, st.uses(u) + 1)
                h_hi(0, 0)
                with steps.loop(1, ROUNDS - 1, f"ffn{st.position}_a") as i:
                    split(d, st.uses(d) + i - 1)
                    silu(i)
                    split(g, st.uses(g) + i + 1)
                    split(u, st.uses(u) + i + 1)
                    h_hi(i, 0)
                i = ROUNDS - 1
                split(d, st.uses(d) + i - 1)
                silu(i)
                split(g, st.uses(g) + ROUNDS)
                h_hi(i, 1)
                if not last_stage:
                    split(u, st.uses(u) + ROUNDS)

            def mix1(st):
                sizes = [KT * w for _, w in MIX1_COLS[:-2]] + [HALF_KT * w for _, w in MIX1_COLS[-2:]] + [UNIT] * OUT_UNITS
                rows_hi(st)
                for job in MIX1_WALK:
                    if job[0] == "unit":
                        m = job[1]
                        split_unit(st, m + 2, sizes)
                        slot, use = st.unit(m)
                        act.wait_ge(used[slot], use + 2)
                        c, w = MIX1_COLS[m]
                        if m == MIX1_PROJ - 2:
                            continue
                        if m == MIX1_PROJ - 1:
                            src = ps[:, 4:4 + TT, 0:w]
                        else:
                            src = bank(4 + m % 2).rearrange("p (t n) -> p t n", t=TT)[:, :, 0:w]
                        dst = rows1[:, :, c:c + w]
                        if m < 2:
                            src = src.rearrange("p t (j d) -> p t j d", j=4)
                            dst = rows1[:, :, QA:KA].rearrange("p t (j f d) -> p t j f d", j=4, f=2)[:, :, :, m, :]
                        act.activation(dst, src, ACT.Silu if c >= GR else ACT.Copy).then_inc(sg["proj_copied"], 1)
                    elif job[0] == "trqk":
                        for i in range(TT):
                            turn_copy(st, TURNS1, job, q1_t[:, :, i * P:(i + 1) * P], HALF, i)
                        turn_copy(st, TURNS1, job, k1_t, S, 2)
                    elif job[0] == "score":
                        attend_probs(st, "W", job[1], TURNS1)
                    elif job[0] == "turn":
                        attend_copy(st, TURNS1, "W", job[1])
                    elif job[0] == "trret":
                        dst, i = (qr_t, kr_t)[job[1] // 2], job[1] % 2
                        turn_copy(st, TURNS1, job, dst[:, :, i * P:(i + 1) * P], HALF)
                    elif job[0] == "attn_out":
                        act.wait_ge(sg["sink_sum"], st.before("sink_sum") + 1)
                        act.activation(sink_e[:, :, :], sink_e[:, :, :], ACT.Exp).then_inc(sg["sink_exp"], 1)
                    elif job[0] == "ycols":
                        y_hi(st, TURNS1, job, YPARTS1)
                    elif job == ("out", 0):
                        split_unit(st, MIX1_PROJ + 2, sizes)
                    elif job == ("out", 2):
                        split_unit(st, MIX1_PROJ + 3, sizes)
                        split_unit(st, MIX1_PROJ + 4, sizes)

            def mix2(st):
                sizes = []
                for unit in MIX2_UNITS:
                    if unit[0] in ("T", "N"):
                        sizes.append(KT * sum(w for _, w in unit[1]))
                    else:
                        sizes.append((6 if unit[0] == "UQ" else 2) * 192)
                sizes += [UNIT] * OUT_UNITS
                pieces = lambda m: {2: (k_piece, 16 * (st.layer + 1)), 3: (w_piece, 32 * (st.layer + 1))}.get(m)
                rows_hi(st)
                for job in MIX2_WALK:
                    if job[0] == "unit":
                        m = job[1]
                        unit = MIX2_UNITS[m]
                        split_unit(st, m + 2, sizes, pieces)
                        slot, use = st.unit(m)
                        act.wait_ge(used[slot], use + 2)
                        src = bank(4 + m % 2).rearrange("p (t n) -> p t n", t=TT)
                        if unit[0] == "T":
                            n = sum(w for _, w in unit[1]) // P
                            dst, src = cols2[:, unit[2]:unit[2] + n, :], src[:, 0:n, :]
                        elif unit[0] == "N":
                            w = sum(w for _, w in unit[1])
                            dst, src = rows2[:, :, unit[2]:unit[2] + w], src[:, :, 0:w]
                        elif unit[0] == "UK":
                            dst = ka[:, :, 3 * unit[1]:3 * unit[1] + 3, 0:HD]
                            src = src[:, :, 0:192].rearrange("p t (h d) -> p t h d", h=3)
                        else:
                            c = (R_QA if unit[0] == "UQ" else R_VA) + 192 * unit[1]
                            dst, src = rows2[:, :, c:c + 192], src[:, :, 0:192]
                        act.activation(dst, src, ACT.Copy).then_inc(sg["proj_copied"], 1)
                    elif job[0] == "idx":
                        i, pairs = IDX_STEPS[job[1]]
                        if job[1] > 0:
                            act.wait_ge(sg["idx_summed"], st.before("idx_summed") + job[1])
                        n = len(pairs) * (i + 1) * P
                        for half in range(2):
                            act.wait_ge(sg["scores"], st.before("scores") + 2 * job[1] + half + 1)
                            act.activation(prob[:, half, 0:n], bank(half, n), ACT.Relu).then_inc(sg["score_free"], 1)
                    elif job[0] == "latent":
                        act.wait_ge(sg["proj_copied"], st.before("proj_copied") + UNITS_LATENT)
                        act.wait_ge(sg["h_ready"], st.before("h_ready"))
                        junk = mod[:, 0:D]
                        for i in range(TT):
                            steps.wait(act.activation(junk[:, 0:Q_LORA], rows2[:, i, R_CQ:R_CKV], ACT.Square,
                                                      accum_out=lat_var[:, 0, i:i + 1]))
                            last = act.activation(junk[:, 0:KV_LORA], rows2[:, i, R_CKV:R_CKV + KV_LORA], ACT.Square,
                                                  accum_out=lat_var[:, 1, i:i + 1])
                            if i < TT - 1:
                                steps.wait(last)
                        last.then_inc(sg["squares"], 1)
                    elif job[0] == "trlat":
                        i, hf = job[1] // 2, job[1] % 2
                        b = turn_wait(st, TURNS2, job)
                        act.activation(lat_hi[:, 4 * hf:4 * hf + 4, i * P:(i + 1) * P],
                                       bank(6 + b).rearrange("p (k s) -> p k s", k=4), ACT.Copy)\
                           .then_inc(sg["hi_part"], 1)
                    elif job[0] == "trA":
                        g = job[1]
                        dst = (qa_t if g < 3 else ka_t)[0:A_HD, 2 * (g % 3):2 * (g % 3) + 2, :]
                        turn_copy(st, TURNS2, job, dst.rearrange("p a b -> p (a b)"), HALF, rows=A_HD)
                    elif job[0] == "score":
                        attend_probs(st, *job[1:], TURNS2)
                    elif job[0] == "turn":
                        attend_copy(st, TURNS2, *job[1:])
                    elif job[0] == "gates":
                        act.wait_ge(sg["proj_copied"], st.before("proj_copied") + MIX2_PROJ)
                        act.activation(rows2[:, :, R_GATE:R_GATE + D], rows2[:, :, R_GATE:R_GATE + D], ACT.Silu)\
                           .then_inc(sg["gates"], 1)
                    elif job[0] == "ycols":
                        y_hi(st, TURNS2, job, YPARTS2)
                    elif job[0] == "out" and job[1] < OUT_UNITS - 2:
                        split_unit(st, MIX2_PROJ + job[1] + 2, sizes)

            for j in range(SLOTS):
                act.sem_inc(hi_ready[j], 1)
            act.wait_ge(c_in, 16)
            act.activation(c_silu, c_raw, ACT.Silu).then_inc(c_ready, 1)
            with steps.loop(0, DEPTH, "layer1_a") as l:
                for pos, name in enumerate(STAGES1):
                    st = Stage(1, l, pos)
                    if name == "ffn":
                        ffn(st, last_stage=pos > 0)
                    if name == "mix1":
                        mix1(st)
            with steps.loop(0, DEPTH, "layer2_a") as l:
                st = Stage(2, l, 0)
                act.wait_ge(mod_stored, 16 * DEPTH * MOD_CHUNKS)
                act.wait_ge(sg["mixed"], st.before("mixed"))
                steps.settle()
                act.dma_start(mod[:, 0:2 * D], mod_rows[l, 0:2 * D].partition_broadcast(P)).then_inc(mod_in, 16)
                mix2(Stage(2, l, 1))

        @block.vector
        def _(dve):
            steps = Steps(dve, v_steps, v_marks)
            tt, stt, ts = dve.tensor_tensor, dve.scalar_tensor_tensor, dve.tensor_scalar

            def split(slot, use, n=UNIT):
                dve.wait_ge(hi_ready[slot], use + 2)
                tt(w_lo[slot][:, 0:n], raw[slot][:, 0:n], w_hi[slot][:, 0:n].bitcast(F32), ALU.subtract)\
                    .then_inc(lo_ready[slot], 1)

            def split_unit(st, m, sizes):
                if m < len(sizes):
                    split(*st.unit(m), sizes[m])
                elif m == len(sizes) and st.block == 1:
                    split(*st.unit(m))

            def lo_part(st, nth, src, hi, lo, b):
                dve.wait_ge(sg["hi_part"], st.before("hi_part") + nth + 1)
                tt(lo, src, hi.bitcast(F32), ALU.subtract).then_inc(free[b], 1)

            def tile_lo(st, i):
                for hf in range(2):
                    tiles, toks = slice(4 * hf, 4 * hf + 4), slice(i * P, (i + 1) * P)
                    lo_part(st, 2 * i + hf, bank(6 + hf).rearrange("p (k s) -> p k s", k=4),
                            col_hi[:, tiles, toks], col_lo[:, tiles, toks], hf)

            def rows_lo(st):
                if st.position in (0, 1) and st.block * st.position != 1:
                    tile_lo(st, 0)
                    split(*st.unit(0))
                tile_lo(st, 1)
                split(*st.unit(1))

            def y_lo(st, job, parts, nth):
                _, i, part = job
                tiles, toks = slice(parts[part][0], parts[part][-1] + 1), slice(i * P, (i + 1) * P)
                lo_part(st, nth, bank(6 + i, len(parts[part]) * P).rearrange("p (k s) -> p k s", s=P),
                        col_hi[:, tiles, toks], col_lo[:, tiles, toks], i)

            def norm(st, banks, params, following=None):
                for i in range(TT):
                    dve.wait_ge(sg["sum_ready"], st.before("sum_ready") - TT + i + 1)
                    total = ps[:, banks[i]:banks[i] + 2, :]
                    xi = x[:, i, :].rearrange("p (a b) -> p a b", a=2)
                    yi = y[:, i, :].rearrange("p (a b) -> p a b", a=2)
                    if st.block == 2:
                        if i == 0:
                            dve.wait_ge(gate_in, 16 * (st.layer + 1))
                        gate = mod[:, 2 * D:3 * D].rearrange("p (a b) -> p a b", a=2)
                        steps.wait(stt(yi, gate, 1.0, total, ALU.add, ALU.mult))
                        total = yi
                    steps.wait(stt(yi, xi, ALPHA, total, ALU.mult, ALU.add))
                    dve.bn_stats(stats[:, i, 0, :], y[:, i, 0:HALF])
                    steps.wait(dve.bn_stats(stats[:, i, 1, :], y[:, i, HALF:D]))
                    steps.settle()
                    steps.wait(dve.bn_aggr(mean_var[:, i, :], stats[:, i, :, :]))
                    ts(mean_var[:, i, 1:2], mean_var[:, i, 1:2], LN_EPS, None, ALU.add).then_inc(sg["var_ready"], 1)
                    if i == 0:
                        dve.wait_ge(params_in, params)
                    elif following is not None:
                        tile_lo(following, 0)
                    steps.wait(stt(y[:, i, :], y[:, i, :], mean_var[:, i, 0:1], norm_g[:, :], ALU.subtract, ALU.mult))
                    dve.wait_ge(sg["rstd_ready"], st.before("rstd_ready") + i + 1)
                    stt(x[:, i, :], y[:, i, :], rstd[:, i:i + 1], norm_b[:, :], ALU.mult, ALU.add)\
                        .then_inc(sg["x_ready"], 1)

            def ffn(st, last_stage=False):
                g, u, d = st.first, (st.first + 1) % SLOTS, (st.first + 2) % SLOTS
                rows_lo(st)

                def h(i):
                    dve.wait_ge(sg["silu_done"], st.before("silu_done") + i + 1)
                    dve.wait_ge(used[u], st.uses(u) + i + 2)
                    if not isinstance(i, int) or i > 0:
                        dve.wait_ge(sg["h_lo"], st.before("h_lo") + i)
                    stt(hidden, silu_a, 0.5, bank(5), ALU.mult, ALU.mult).then_inc(sg["h_done"], 1)

                def h_lo(i, s_):
                    dve.wait_ge(sg["h_hi"], st.before("h_hi") + i + 1)
                    tiles = slice(2 * s_, 2 * s_ + 2)
                    tt(lat_lo[:, tiles, :].rearrange("p a b -> p (a b)"), hidden,
                       lat_hi[:, tiles, :].rearrange("p a b -> p (a b)").bitcast(F32), ALU.subtract)\
                        .then_inc(sg["h_lo"], 1)

                chunks = st.before("mod_summed") - 2

                def mod_sum(i):
                    dve.wait_ge(ada_in, 16 * (chunks + i + 1))
                    steps.wait(ts(ada_sum, ada_w[:, 0, :], c_silu[:, 0:1], None, ALU.mult))
                    for k in range(1, KT):
                        last = stt(ada_sum, ada_w[:, k, :], c_silu[:, k:k + 1], ada_sum, ALU.mult, ALU.add)
                        if k < KT - 1:
                            steps.wait(last)
                    last.then_inc(sg["mod_summed"], 1)

                def mod_row(i):
                    dve.wait_ge(sg["mod_spread"], chunks + i + 1)
                    dve.wait_ge(ada_bias_in, 16 * (chunks + i + 1))
                    tt(ada_row, ps[0:1, 6, 0:MOD_W], ada_bias, ALU.add).then_inc(sg["mod_row"], 1)

                def body(i, chunk):
                    split(d, st.uses(d) + i - 1)
                    if chunk:
                        mod_sum(i)
                    split(g, st.uses(g) + i + 1)
                    h(i)
                    split(u, st.uses(u) + i + 1)
                    h_lo(i, 0)
                    if chunk:
                        mod_row(i)

                split(g, st.uses(g) + 1)
                h(0)
                split(u, st.uses(u) + 1)
                h_lo(0, 0)
                body(1, False)
                with steps.loop(2, ROUNDS - 1, f"ffn{st.position}_v") as i:
                    body(i, True)
                i = ROUNDS - 1
                split(d, st.uses(d) + i - 1)
                split(g, st.uses(g) + ROUNDS)
                h(i)
                h_lo(i, 1)
                if not last_stage:
                    split(u, st.uses(u) + ROUNDS)

            def rope(x1, x2, whole, cos, sin, shape, cos_whole, tmp1, tmp2):
                tt(tmp1, x2, sin.to_broadcast(shape), ALU.mult)
                steps.wait(tt(tmp2, x1, sin.to_broadcast(shape), ALU.mult))
                steps.wait(tt(whole, whole, cos_whole, ALU.mult))
                tt(x1, x1, tmp1, ALU.subtract)
                return tt(x2, x2, tmp2, ALU.add)

            def attend_max(st, group, s):
                _, i, pairs = steps_of(group)[s]
                o_, before, keys, n = ordinal(group, s), scored_before(group, s), (i + 1) * P, len(pairs)
                if o_ > 0:
                    dve.wait_ge(sg["probs"], st.before("probs") + o_)
                scale = A_HD ** -0.5 if group == "A" else HD ** -0.5
                window = slice(2 * P - keys, 2 * P)
                for half in range(2):
                    dve.wait_ge(sg["scores"], st.before("scores") + 2 * before + half + 1)
                    if group in "WA":
                        bias = table[:, 0:256][:, window].unsqueeze(1).to_broadcast([P, n, keys])
                    else:
                        at_, per = (T2_B, 3) if group == "B" else (T2_C, 2)
                        bias = table[:, at_ + half * per * 256:at_ + (half + 1) * per * 256]\
                            .rearrange("p (j s) -> p j s", j=per)[:, pairs[0]:pairs[-1] + 1, window]
                    dst = score[:, half, 0:n * keys].rearrange("p (j s) -> p j s", j=n)
                    last = stt(dst, bank(half, n * keys).rearrange("p (j s) -> p j s", j=n), scale, bias,
                               ALU.mult, ALU.add)
                    last.then_inc(sg["score_free"], 1)
                    dve.wait_ge(sg["score_free"], st.before("score_free") + 2 * before + half + 1)
                    if group == "C":
                        steps.wait(tt(dst, dst, not_taken[:, i, 0:keys].unsqueeze(1).to_broadcast([P, n, keys]),
                                      ALU.add))
                steps.wait(dve.tensor_reduce(by_pair(row_max, i, group, pairs),
                                             score[:, :, 0:n * keys].rearrange("p f (j s) -> p f j s", j=n),
                                             AX_X, ALU.max))
                top = by_pair(row_max, i, group, pairs)
                if group == "W":
                    steps.wait(tt(top, top, sinks.rearrange("p (f j) -> p f j", f=2)[:, :, pairs[0]:pairs[-1] + 1],
                                  ALU.max))
                ts(by_pair(neg_max, i, group, pairs), top, -1.0, None, ALU.mult).then_inc(sg["maxed"], 1)

            def read_out(st, group, i, col, signal):
                heads = group_heads(group)
                steps.wait(dve.reciprocal(row_inv[:, i, 0:heads], row_sum[:, i, 0:heads]))
                return tt(y[:, i, col:col + heads * HD].rearrange("p (h d) -> p h d", h=heads),
                          bank(2 + i, heads * HD).rearrange("p (h d) -> p h d", h=heads),
                          row_inv[:, i, 0:heads].unsqueeze(2).to_broadcast([P, heads, HD]), ALU.mult)

            def mix1(st):
                sizes = [KT * w for _, w in MIX1_COLS[:-2]] + [HALF_KT * w for _, w in MIX1_COLS[-2:]] + [UNIT] * OUT_UNITS
                rows_lo(st)
                for job in MIX1_WALK:
                    if job[0] == "unit":
                        split_unit(st, job[1] + 2, sizes)
                    elif job[0] == "rope1":
                        dve.wait_ge(sg["proj_copied"], st.before("proj_copied") + 3)
                        heads = ATTN1_HEADS + KV1_HEADS
                        for i in range(TT):
                            v = rows1[:, i, QA:VA].rearrange("p (h f d) -> p h f d", h=heads, f=2)
                            cos, sin = (table[:, T1_ROPE + 64 * i + c:T1_ROPE + 64 * i + c + 32] for c in (0, 32))
                            tmp = score[:, :, 0:320].rearrange("p f (h d) -> p f h d", h=heads)
                            tmp = [tmp[:, f, :, :] for f in range(2)]
                            last = rope(v[:, :, 0, :], v[:, :, 1, :], v, None, sin.unsqueeze(1), [P, heads, 32],
                                        cos.unsqueeze(1).unsqueeze(1).to_broadcast([P, heads, 2, 32]), *tmp)
                            if i < TT - 1:
                                steps.wait(last)
                        last.then_inc(sg["rope_done"], 1)
                    elif job[0] == "score":
                        if job[1] == 0:
                            dve.wait_ge(sinks_in, 16 * (st.layer + 1))
                        attend_max(st, "W", job[1])
                    elif job[0] == "attn_out":
                        dve.wait_ge(sg["probs"], st.before("probs") + 3)
                        tt(sink_e[:, :, :], neg_max[:, :, :], sinks.unsqueeze(1).to_broadcast([P, TT, 8]), ALU.add)\
                            .then_inc(sg["sink_sum"], 1)
                        dve.wait_ge(sg["sink_exp"], st.before("sink_exp") + 1)
                        steps.wait(tt(row_sum[:, :, :], row_sum[:, :, :], sink_e[:, :, :], ALU.add))
                        dve.wait_ge(sg["mixed"], st.before("mixed") + 3)
                        for i in range(TT):
                            read_out(st, "W", i, 0, None).then_inc(sg["out_copied"], 1)
                        dve.wait_ge(sg["out_copied"], st.before("out_copied") + TT)
                        dve.sem_inc(sg["y_ready"], TT)
                    elif job[0] == "ret":
                        j = job[1]
                        decayed = prob if j % 2 == 0 else score
                        if j >= 2:
                            dve.wait_ge(sg["ret_mixed"], st.before("ret_mixed") + j - 1)
                        decay = table[:, T1_DECAY:T1_ROPE].rearrange("p (f j s) -> p f j s", f=2, j=4)
                        dve.wait_ge(sg["scores"], st.before("scores") + 2 * (3 + j) + 2)
                        tt(decayed[:, :, 0:S], ps[:, 0:2, 0:S], decay[:, :, j, :], ALU.mult)
                        tt(decayed[:, :, S:S + P], ps[:, 0:2, S:S + P], decay[:, :, j, 0:P], ALU.mult)\
                            .then_inc(sg["score_free"], 2)
                    elif job[0] == "groupnorm":
                        dve.wait_ge(sg["ret_mixed"], st.before("ret_mixed") + 4)
                        dve.wait_ge(sg["proj_copied"], st.before("proj_copied") + MIX1_PROJ - 1)
                        heads = lambda v: v.rearrange("p (h d) -> p h d", h=8)
                        wide = lambda v: v.unsqueeze(2).to_broadcast([P, 8, HD])
                        square = heads(score[:, 0, :])
                        for i in range(TT):
                            o_, yr = heads(bank(2 + i)), heads(y[:, i, HALF:D])
                            steps.wait(dve.tensor_reduce(gn_sum[:, i, :], o_, AX_X, ALU.add))
                            steps.wait(ts(gn_sum[:, i, :], gn_sum[:, i, :], 1.0 / HD, None, ALU.mult))
                            steps.wait(tt(yr, o_, wide(gn_sum[:, i, :]), ALU.subtract))
                            steps.wait(tt(square, yr, yr, ALU.mult))
                            steps.wait(dve.tensor_reduce(gn_var[:, i, :], square, AX_X, ALU.add))
                            ts(gn_var[:, i, :], gn_var[:, i, :], 1.0 / HD, GN_EPS, ALU.mult, ALU.add)\
                                .then_inc(sg["var_ready"], 1)
                            steps.wait(tt(yr, yr, heads(rows1[:, i, GR:IN1]), ALU.mult))
                        for i in range(TT):
                            yr = heads(y[:, i, HALF:D])
                            dve.wait_ge(sg["rstd_ready"], st.before("rstd_ready") + i + 1)
                            tt(yr, yr, wide(gn_rstd[:, i, :]), ALU.mult).then_inc(sg["y_ready"], 1)
                    elif job[0] == "ycols":
                        y_lo(st, job, YPARTS1, 2 * TT + 2 * job[2] + job[1])
                    elif job == ("out", 0):
                        split_unit(st, MIX1_PROJ + 2, sizes)
                    elif job == ("out", 2):
                        split_unit(st, MIX1_PROJ + 3, sizes)
                        split_unit(st, MIX1_PROJ + 4, sizes)

            def condition(st):
                dve.wait_ge(mod_in, 16 * (st.layer + 1))
                for i in range(TT):
                    steps.wait(stt(y[:, i, :], mod[:, D:2 * D], 1.0, x[:, i, :], ALU.add, ALU.mult))
                    tt(y[:, i, :], y[:, i, :], mod[:, 0:D], ALU.add).then_inc(sg["h_ready"], 1)

            def mix2(st):
                sizes = []
                for unit in MIX2_UNITS:
                    if unit[0] in ("T", "N"):
                        sizes.append(KT * sum(w for _, w in unit[1]))
                    else:
                        sizes.append((6 if unit[0] == "UQ" else 2) * 192)
                sizes += [UNIT] * OUT_UNITS
                rows_lo(st)
                y_jobs = [j for j in MIX2_WALK if j[0] == "ycols"]
                for job in MIX2_WALK:
                    if job[0] == "unit":
                        split_unit(st, job[1] + 2, sizes)
                    elif job[0] == "idxw":
                        dve.wait_ge(sg["proj_copied"], st.before("proj_copied") + UNITS_IDX_W)
                        steps.wait(ts(idx_w[:, :, :], rows2[:, :, R_WI:R_WI + 8], IDX_HEADS ** -0.5 * 64 ** -0.5,
                                      None, ALU.mult))
                        dve.wait_ge(tables_in, 32)
                        for i in range(TT):
                            keys = (i + 1) * P
                            last = dve.tensor_copy(idx_score[:, i, 0:keys], table[:, 2 * P - keys:2 * P])
                        steps.wait(last)
                    elif job[0] == "idx":
                        i, pairs = IDX_STEPS[job[1]]
                        keys = (i + 1) * P
                        for half in range(2):
                            dve.wait_ge(sg["score_free"], st.before("score_free") + 2 * job[1] + half + 1)
                            for n, j in enumerate(pairs):
                                h = 2 * j + half
                                last = stt(idx_score[:, i, 0:keys], prob[:, half, n * keys:(n + 1) * keys],
                                           idx_w[:, i, h:h + 1], idx_score[:, i, 0:keys], ALU.mult, ALU.add)
                                if (half, j) != (1, pairs[-1]):
                                    steps.wait(last)
                        last.then_inc(sg["idx_summed"], 1)
                    elif job[0] == "topk":
                        _, i, part = job
                        keys = (i + 1) * P
                        if (i, part) == (0, 0):
                            dve.wait_ge(sg["idx_summed"], st.before("idx_summed") + 3)
                        cur = idx_score[:, i, 0:keys]
                        for _ in range(TOPK // 8 // TOPK_PARTS):
                            steps.settle()
                            steps.wait(dve.max(top8, cur))
                            steps.settle()
                            steps.wait(dve.match_replace(cur, top8, cur, TAKEN))
                        if part == TOPK_PARTS - 1:
                            steps.wait(ts(not_taken[:, i, 0:keys], cur, TAKEN / 2, NEG, ALU.is_gt, ALU.mult))
                    elif job[0] == "latent":
                        dve.wait_ge(sg["squares"], st.before("squares") + 1)
                        ts(lat_var[:, 0, :], lat_var[:, 0, :], 1.0 / Q_LORA, RMS_EPS, ALU.mult, ALU.add)
                        ts(lat_var[:, 1, :], lat_var[:, 1, :], 1.0 / KV_LORA, RMS_EPS, ALU.mult, ALU.add)\
                            .then_inc(sg["var_ready"], 1)
                        dve.wait_ge(sg["rstd_ready"], st.before("rstd_ready") + 1)
                        dve.wait_ge(lat_g_in, 32 * (st.layer + 1))
                        for i in range(TT):
                            for a, (c, n) in enumerate(((R_CQ, Q_LORA), (R_CKV, KV_LORA))):
                                last = stt(rows2[:, i, c:c + n], rows2[:, i, c:c + n], lat_rstd[:, a, i:i + 1],
                                           norm_b[:, c:c + n], ALU.mult, ALU.mult)
                                if a == 0:
                                    steps.wait(last)
                            last.then_inc(sg["latent"], 1)
                    elif job[0] == "trlat":
                        i, hf = job[1] // 2, job[1] % 2
                        tiles, toks = slice(4 * hf, 4 * hf + 4), slice(i * P, (i + 1) * P)
                        b = TURNS2[job][0][0]
                        lo_part(st, 2 * TT + job[1], bank(6 + b).rearrange("p (k s) -> p k s", k=4),
                                lat_hi[:, tiles, toks], lat_lo[:, tiles, toks], b)
                    elif job[0] == "ropeA":
                        dve.wait_ge(sg["proj_copied"], st.before("proj_copied") + UNITS_UQ)
                        for i in range(TT):
                            cos, sin = (table[:, T2_ROPE + 32 * i + c:T2_ROPE + 32 * i + c + 16] for c in (0, 16))
                            q = rows2[:, i, R_QA:R_QA + A_HEADS * A_HD].rearrange("p (h d) -> p h d", h=A_HEADS)
                            q = q[:, :, A_NOPE:A_HD].rearrange("p h (f d) -> p h f d", f=2)
                            tmp = rope_tmp[:, 0:192].rearrange("p (f h d) -> p f h d", f=2, h=A_HEADS)
                            last = rope(q[:, :, 0, :], q[:, :, 1, :], q, None, sin.unsqueeze(1), [P, A_HEADS, 16],
                                        cos.unsqueeze(1).unsqueeze(1).to_broadcast([P, A_HEADS, 2, 16]),
                                        tmp[:, 0, :, :], tmp[:, 1, :, :])
                            if i < TT - 1:
                                steps.wait(last)
                        last.then_inc(sg["rope_done"], 1)
                    elif job[0] == "ropeK":
                        for i in range(TT):
                            cos, sin = (table[:, T2_ROPE + 32 * i + c:T2_ROPE + 32 * i + c + 16] for c in (0, 16))
                            k = rows2[:, i, R_KR:R_KR + A_ROPE].rearrange("p (f d) -> p f d", f=2)
                            steps.wait(rope(k[:, 0, :], k[:, 1, :], k, None, sin, [P, 16],
                                            cos.unsqueeze(1).to_broadcast([P, 2, 16]),
                                            rope_tmp[:, 0:16], rope_tmp[:, 16:32]))
                            last = dve.tensor_copy(ka[:, i, :, A_NOPE:A_HD],
                                                   rows2[:, i, R_KR:R_KR + A_ROPE].unsqueeze(1)
                                                   .to_broadcast([P, A_HEADS, A_ROPE]))
                        steps.wait(last)
                    elif job[0] == "score":
                        attend_max(st, *job[1:])
                    elif job[0] == "mix":
                        group, s = job[1:]
                        if s in (0, len(STEPS2[group]) - 1):
                            i = 0 if s == 0 else 1
                            dve.wait_ge(sg["mixed"], st.before("mixed") + ORDER2[group, s] + 1)
                            col = {"A": 0, "B": 384, "C": 768}[group]
                            read_out(st, group, i, col, None).then_inc(sg["out_copied"], 1)
                    elif job[0] == "ycols":
                        _, i, part = job
                        nth = y_jobs.index(job)
                        if nth == 0:
                            dve.wait_ge(sg["gates"], st.before("gates") + 1)
                            dve.wait_ge(sg["out_copied"], st.before("out_copied") + 6)
                        for _, g_i, g_part in y_jobs[:3] if nth == 0 else y_jobs[nth + 2:nth + 3]:
                            cols = slice(YPARTS2[g_part][0] * P, (YPARTS2[g_part][-1] + 1) * P)
                            tt(y[:, g_i, cols], y[:, g_i, cols], rows2[:, g_i, R_GATE:R_GATE + D][:, cols], ALU.mult)\
                                .then_inc(sg["y_ready"], 1)
                        y_lo(st, job, YPARTS2, 2 * TT + 4 + y_jobs.index(job))
                    elif job[0] == "out" and job[1] < OUT_UNITS - 2:
                        split_unit(st, MIX2_PROJ + job[1] + 2, sizes)

            for j in range(SLOTS):
                dve.sem_inc(lo_ready[j], 1)
            for b in range(2):
                dve.sem_inc(free[b], 1)
            dve.memset(minus_half, -0.5).then_inc(const_ready, 1)
            dve.memset(ones[:, :], 1.0).then_inc(const_ready, 1)
            dve.wait_ge(c_ready, 1)
            dve.wait_ge(x_landed, 16)
            dve.sem_inc(sg["x_ready"], TT)
            dve.wait_ge(tables_in, 16)
            with steps.loop(0, DEPTH, "layer1_v") as l:
                for pos, name in enumerate(STAGES1):
                    st = Stage(1, l, pos)
                    if name == "ffn":
                        ffn(st, last_stage=pos > 0)
                    elif name == "mix1":
                        mix1(st)
                    else:
                        norm(st, (4, 0) if STAGES1[pos - 1] == "mix1" else (0, 2), 32 * (3 * l + pos // 2 + 1),
                             Stage(1, l, pos + 1) if pos + 1 < len(STAGES1) else None)
            with steps.loop(0, DEPTH, "layer2_v") as l:
                condition(Stage(2, l, 0))
                mix2(Stage(2, l, 1))
                norm(Stage(2, l, 2), (4, 0), 32 * (3 * DEPTH + l + 1))

        @block.gpsimd
        def _(pool):
            steps = Steps(pool, g_steps, p_marks)

            def params(l, g, b):
                steps.settle()
                pool.dma_start(norm_g[:, :], g[l].partition_broadcast(P)).then_inc(params_in, 16)
                pool.dma_start(norm_b[:, :], b[l].partition_broadcast(P)).then_inc(params_in, 16)

            def norm(st):
                for i in range(TT):
                    pool.wait_ge(sg["var_ready"], st.before("var_ready") + i + 1)
                    pool.tensor_tensor(rstd[:, i:i + 1], mean_var[:, i, 1:2], minus_half[:, 0:1], ALU.pow)\
                        .then_inc(sg["rstd_ready"], 1)

            def mod_stream(st, l, first):
                before = st.before("mod_summed")

                def chunk_in(i):
                    steps.settle()
                    pool.dma_start(ada_w, t["w_ada_2"][l, :, bass.ds((i + first) * MOD_W, MOD_W)]
                                   .rearrange("(k p) n -> p k n", p=P)).then_inc(ada_in, 16)

                def bias_in(i):
                    pool.dma_start(ada_bias, t["b_ada_2"][l, bass.ds((i + first) * MOD_W, MOD_W)]
                                   .partition_broadcast(1)).then_inc(ada_bias_in, 16)

                def row_out(i):
                    pool.wait_ge(sg["mod_row"], before + i + 1)
                    steps.settle()
                    pool.dma_start(mod_rows[l, bass.ds((i + first) * MOD_W, MOD_W)].partition_broadcast(1), ada_row)\
                        .then_inc(mod_stored, 16)
                    pool.wait_ge(mod_stored, 16 * (before + i + 1))
                    steps.settle()

                chunk_in(0)
                bias_in(0)
                with steps.loop(1, MOD_CHUNKS // 2, f"mod{st.position}_g") as i:
                    pool.wait_ge(sg["mod_summed"], before + i)
                    chunk_in(i)
                    row_out(i - 1)
                    bias_in(i)
                row_out(MOD_CHUNKS // 2 - 1)

            def rotate(st):
                pool.wait_ge(sg["proj_copied"], st.before("proj_copied") + 7)
                heads = 2 * RET_HEADS
                for i in range(TT):
                    v = rows1[:, i, QR:VR].rearrange("p (h d f) -> p h d f", h=heads, f=2)
                    cos, sin = (table[:, T1_RET + 64 * i + c:T1_RET + 64 * i + c + 32] for c in (0, 32))
                    tmp = rot_tmp.rearrange("p (f h d) -> p f h d", f=2, h=heads)
                    wide = lambda a: a.unsqueeze(1).to_broadcast([P, heads, 32])
                    pool.tensor_tensor(tmp[:, 0, :, :], v[:, :, :, 1], wide(sin), ALU.mult)
                    steps.wait(pool.tensor_tensor(tmp[:, 1, :, :], v[:, :, :, 0], wide(sin), ALU.mult))
                    pool.tensor_tensor(v[:, :, :, 0], v[:, :, :, 0], wide(cos), ALU.mult)
                    steps.wait(pool.tensor_tensor(v[:, :, :, 1], v[:, :, :, 1], wide(cos), ALU.mult))
                    pool.tensor_tensor(v[:, :, :, 0], v[:, :, :, 0], tmp[:, 0, :, :], ALU.subtract)
                    last = pool.tensor_tensor(v[:, :, :, 1], v[:, :, :, 1], tmp[:, 1, :, :], ALU.add)
                    if i < TT - 1:
                        steps.wait(last)
                last.then_inc(sg["rotated"], 1)

            pool.dma_start(ident[:, :], t["ident"]).then_inc(ident_in, 16)
            pool.dma_start(c_raw, t["c_2"][0].rearrange("(k p) -> p k", p=P),
                           allow_slow_non_contiguous=True).then_inc(c_in, 16)
            pool.dma_start(x[:, :, :], t["x"][0].rearrange("(t p) d -> p t d", p=P)).then_inc(x_landed, 16)
            pool.dma_start(table[:, 0:T1], t["table1"]).then_inc(tables_in, 16)
            pool.wait_ge(const_ready, 2)
            with steps.loop(0, DEPTH, "layer1_g") as l:
                for pos, name in enumerate(STAGES1):
                    st = Stage(1, l, pos)
                    if name in ("ffn", "mix1"):
                        pool.wait_ge(sg["x_ready"], st.before("x_ready") + TT)
                        n = pos // 2 + 1
                        params(l, t[f"ln{n}_g"], t[f"ln{n}_b"])
                    if name == "ffn":
                        mod_stream(st, l, 0 if pos == 0 else MOD_CHUNKS // 2)
                    if name == "mix1":
                        pool.dma_start(sinks, t["attn_sinks"][l].partition_broadcast(P)).then_inc(sinks_in, 16)
                        rotate(st)
                        for i in range(TT):
                            pool.wait_ge(sg["var_ready"], st.before("var_ready") + i + 1)
                            pool.tensor_tensor(gn_rstd[:, i, :], gn_var[:, i, :], minus_half, ALU.pow)\
                                .then_inc(sg["rstd_ready"], 1)
                    if name == "norm":
                        norm(st)
            pool.wait_ge(sg["x_ready"], TT + signals_before(2, 0, 0, "x_ready"))
            pool.dma_start(table[:, 0:T2], t["table2"]).then_inc(tables_in, 16)
            with steps.loop(0, DEPTH, "layer2_g") as l:
                st = Stage(2, l, 0)
                pool.wait_ge(mod_stored, 16 * DEPTH * MOD_CHUNKS)
                pool.wait_ge(sg["x_ready"], st.before("x_ready") + TT)
                steps.settle()
                pool.dma_start(mod[:, 2 * D:MOD], mod_rows[l, 2 * D:MOD].partition_broadcast(P)).then_inc(gate_in, 16)
                pool.dma_start(norm_b[:, 0:Q_LORA], t["q_norm_g_2"][l].partition_broadcast(P)).then_inc(lat_g_in, 16)
                pool.dma_start(norm_b[:, Q_LORA:D], t["kv_norm_g_2"][l].partition_broadcast(P)).then_inc(lat_g_in, 16)
                st = Stage(2, l, 1)
                pool.wait_ge(sg["var_ready"], st.before("var_ready") + 1)
                pool.tensor_tensor(lat_rstd, lat_var, minus_half[:, 0:4].rearrange("p (a t) -> p a t", a=2), ALU.pow)\
                    .then_inc(sg["rstd_ready"], 1)
                pool.wait_ge(sg["latent"], st.before("latent") + TT)
                params(l, t["ln_g_2"], t["ln_b_2"])
                norm(Stage(2, l, 2))


def kernel(**inputs):
    import concourse.bacc as bacc
    from concourse.bass_utils import run_bass_kernel_spmd

    nc = bacc.Bacc("TRN2", target_bir_lowering=False, num_devices=1)
    arrays = {f"in_{k}": np.ascontiguousarray(v) for k, v in inputs.items()}
    for name, table in zip(("table1", "table2", "ident"), shape_tables()):
        arrays[f"in_{name}"] = table
    t = {k[3:]: nc.dram_tensor(k, v.shape, mybir.dt.from_np(v.dtype), kind="ExternalInput").ap()
         for k, v in arrays.items()}
    out = nc.dram_tensor("out_0", (1, S, D), F32, kind="ExternalOutput").ap()
    build(nc, t, out)
    result = run_bass_kernel_spmd(nc, [arrays], core_ids=[0])
    return result.results[0]["out_0"]
```
